# Optimizing a Trainium2 kernel written in Bass

```python
import jax, jax.numpy as jnp
from jax import lax
import numpy as np

D_MODEL = 1024
BATCH = 1
SEQ = 1024
DEPTH = 2

QBLOCK = 128
WINDOW = 128
EPS = 1e-6
ROPE_THETA = 10000.0
MLA_HEADS = D_MODEL // 128
MLA_Q_RANK = D_MODEL // 4
MLA_KV_RANK = D_MODEL // 8
MLA_NOPE = 64
MLA_ROPE = 32
MLA_V = 64
SWA_HEADS = D_MODEL // 128
SWA_KV_HEADS = SWA_HEADS // 4
SWA_HEAD_DIM = 64
FOX_HEADS = D_MODEL // 64
FOX_HEAD_DIM = 64
FOX_WIDTH = FOX_HEADS * FOX_HEAD_DIM
FORGET_BIAS_INIT = 2.0

EVEN_WIDTH = MLA_HEADS * MLA_V + SWA_HEADS * SWA_HEAD_DIM
EVEN_SPLITS = (MLA_Q_RANK, MLA_KV_RANK, MLA_ROPE, SWA_HEADS * SWA_HEAD_DIM,
               SWA_KV_HEADS * SWA_HEAD_DIM, SWA_KV_HEADS * SWA_HEAD_DIM, EVEN_WIDTH)
ODD_SPLITS = (FOX_WIDTH, FOX_WIDTH, FOX_WIDTH, FOX_HEADS, FOX_WIDTH)
N_EVEN = (DEPTH + 1) // 2
N_ODD = DEPTH // 2


def rms_norm(x, g):
    xf = x.astype(jnp.float32)
    y = xf * lax.rsqrt(jnp.mean(xf * xf, axis=-1, keepdims=True) + EPS)
    return (y * g.astype(jnp.float32)).astype(x.dtype)

def split_cols(z, sizes):
    idx = [int(v) for v in np.cumsum(sizes)[:-1]]
    return jnp.split(z, idx, axis=-1)

def rope_angles(positions, dim):
    inv_freq = 1.0 / (ROPE_THETA ** (jnp.arange(0, dim, 2, dtype=jnp.float32) / dim))
    return positions.astype(jnp.float32)[..., None] * inv_freq

def apply_rope(x, ang):
    cos, sin = jnp.cos(ang), jnp.sin(ang)
    xf = x.astype(jnp.float32)
    x1, x2 = jnp.split(xf, 2, axis=-1)
    return jnp.concatenate([x1 * cos - x2 * sin, x2 * cos + x1 * sin], axis=-1).astype(x.dtype)

def alibi_slopes(n):
    return 2.0 ** (-8.0 * (jnp.arange(n, dtype=jnp.float32) + 1.0) / n)

def causal_block_attention(q, k, v, log_cum=None):
    B, S, H, Dk = q.shape
    Dv = v.shape[-1]
    nb = S // QBLOCK
    scale = Dk ** -0.5
    kpos = jnp.arange(S)
    lc_t = None if log_cum is None else jnp.transpose(log_cum, (0, 2, 1))

    def one_block(i):
        start = i * QBLOCK
        qi = lax.dynamic_slice_in_dim(q, start, QBLOCK, axis=1)
        s = jnp.einsum('bqhd,bkhd->bhqk', qi, k, preferred_element_type=jnp.float32) * scale
        if lc_t is not None:
            ci = lax.dynamic_slice_in_dim(lc_t, start, QBLOCK, axis=2)
            s = s + ci[..., :, None] - lc_t[..., None, :]
        qpos = start + jnp.arange(QBLOCK)
        mask = kpos[None, :] <= qpos[:, None]
        s = jnp.where(mask, s, -jnp.inf)
        p = jax.nn.softmax(s, axis=-1)
        return jnp.einsum('bhqk,bkhd->bqhd', p.astype(v.dtype), v)

    out = lax.map(one_block, jnp.arange(nb))
    return jnp.transpose(out, (1, 0, 2, 3, 4)).reshape(B, S, H, Dv)

def sliding_window_sink_attention(q, k, v, sinks, slopes):
    B, S, H, D = q.shape
    KV = k.shape[2]
    G = H // KV
    W = WINDOW
    nb = S // W
    qb = q.reshape(B, nb, W, KV, G, D)
    pad = ((0, 0), (W, 0), (0, 0), (0, 0))
    kp = jnp.pad(k, pad).reshape(B, nb + 1, W, KV, D)
    vp = jnp.pad(v, pad).reshape(B, nb + 1, W, KV, D)
    kb = jnp.concatenate([kp[:, :-1], kp[:, 1:]], axis=2)
    vb = jnp.concatenate([vp[:, :-1], vp[:, 1:]], axis=2)
    s = jnp.einsum('bnqkgd,bnckd->bnkgqc', qb, kb, preferred_element_type=jnp.float32) * (D ** -0.5)
    a = jnp.arange(W)[:, None]
    c = jnp.arange(2 * W)[None, :]
    dist = (W + a - c).astype(jnp.float32)
    blk = jnp.arange(nb)[:, None, None]
    valid = (dist >= 0) & (dist < W) & (blk * W + c[None] - W >= 0)
    s = s - slopes.reshape(KV, G)[:, :, None, None] * dist
    s = jnp.where(valid[None, :, None, None], s, -jnp.inf)
    sink = sinks.astype(jnp.float32).reshape(KV, G)[:, :, None, None]
    m = jnp.maximum(jnp.max(s, axis=-1, keepdims=True), sink)
    p = jnp.exp(s - m)
    p = p / (jnp.sum(p, axis=-1, keepdims=True) + jnp.exp(sink - m))
    o = jnp.einsum('bnkgqc,bnckd->bnqkgd', p.astype(v.dtype), vb)
    return o.reshape(B, S, H, D)

def mla_swa_layer(x, positions, g_in, w_in, g_q_a, w_q_up, g_kv_a, w_kv_up, sinks, w_out):
    B, S, _ = x.shape
    h = rms_norm(x, g_in)
    z = h @ w_in
    cq, ckv, kpe, q_s, k_s, v_s, gate = split_cols(z, EVEN_SPLITS)
    q = (rms_norm(cq, g_q_a) @ w_q_up).reshape(B, S, MLA_HEADS, MLA_NOPE + MLA_ROPE)
    q_nope, q_pe = q[..., :MLA_NOPE], q[..., MLA_NOPE:]
    kv = (rms_norm(ckv, g_kv_a) @ w_kv_up).reshape(B, S, MLA_HEADS, MLA_NOPE + MLA_V)
    k_nope, v_m = kv[..., :MLA_NOPE], kv[..., MLA_NOPE:]
    ang = rope_angles(positions, MLA_ROPE)
    q_pe = apply_rope(q_pe, ang[:, :, None, :])
    k_pe = apply_rope(kpe, ang)[:, :, None, :]
    qm = jnp.concatenate([q_nope, q_pe], axis=-1)
    km = jnp.concatenate([k_nope, jnp.broadcast_to(k_pe, (B, S, MLA_HEADS, MLA_ROPE))], axis=-1)
    o_mla = causal_block_attention(qm, km, v_m)
    o_swa = sliding_window_sink_attention(
        q_s.reshape(B, S, SWA_HEADS, SWA_HEAD_DIM),
        k_s.reshape(B, S, SWA_KV_HEADS, SWA_HEAD_DIM),
        v_s.reshape(B, S, SWA_KV_HEADS, SWA_HEAD_DIM),
        sinks, alibi_slopes(SWA_HEADS))
    o = jnp.concatenate([o_mla.reshape(B, S, -1), o_swa.reshape(B, S, -1)], axis=-1)
    return x + (o * jax.nn.silu(gate)) @ w_out

def fox_layer(x, g_in, w_in, b_f, w_out):
    B, S, _ = x.shape
    h = rms_norm(x, g_in)
    z = h @ w_in
    q, k, v, f_logit, gate = split_cols(z, ODD_SPLITS)
    log_f = jax.nn.log_sigmoid(f_logit.astype(jnp.float32) + b_f.astype(jnp.float32))
    log_cum = jnp.cumsum(log_f, axis=1)
    o = causal_block_attention(q.reshape(B, S, FOX_HEADS, FOX_HEAD_DIM),
                               k.reshape(B, S, FOX_HEADS, FOX_HEAD_DIM),
                               v.reshape(B, S, FOX_HEADS, FOX_HEAD_DIM), log_cum=log_cum)
    return x + (o.reshape(B, S, FOX_WIDTH) * jax.nn.silu(gate)) @ w_out

def first_inputs(seed: int = 0) -> dict:
    key = jax.random.key(seed)
    ks = jax.random.split(key, 16)
    f32 = jnp.float32

    def w(k, shape, fan_in):
        return jax.random.normal(k, shape, f32) * (fan_in ** -0.5)

    def gain(k, shape):
        return 1.0 + 0.05 * jax.random.normal(k, shape, f32)

    x = jax.random.normal(ks[0], (BATCH, SEQ, D_MODEL), f32)
    positions = jnp.broadcast_to(jnp.arange(SEQ, dtype=jnp.int32), (BATCH, SEQ))
    return {
        "x": x,
        "positions": positions,
        "e_g_in": gain(ks[1], (N_EVEN, D_MODEL)),
        "e_w_in": w(ks[2], (N_EVEN, D_MODEL, sum(EVEN_SPLITS)), D_MODEL),
        "e_g_q_a": gain(ks[3], (N_EVEN, MLA_Q_RANK)),
        "e_w_q_up": w(ks[4], (N_EVEN, MLA_Q_RANK, MLA_HEADS * (MLA_NOPE + MLA_ROPE)), MLA_Q_RANK),
        "e_g_kv_a": gain(ks[5], (N_EVEN, MLA_KV_RANK)),
        "e_w_kv_up": w(ks[6], (N_EVEN, MLA_KV_RANK, MLA_HEADS * (MLA_NOPE + MLA_V)), MLA_KV_RANK),
        "e_sinks": jax.random.normal(ks[7], (N_EVEN, SWA_HEADS), f32),
        "e_w_out": w(ks[8], (N_EVEN, EVEN_WIDTH, D_MODEL), EVEN_WIDTH),
        "o_g_in": gain(ks[9], (N_ODD, D_MODEL)),
        "o_w_in": w(ks[10], (N_ODD, D_MODEL, sum(ODD_SPLITS)), D_MODEL),
        "o_b_f": FORGET_BIAS_INIT + 0.5 * jax.random.normal(ks[11], (N_ODD, FOX_HEADS), f32),
        "o_w_out": w(ks[12], (N_ODD, FOX_WIDTH, D_MODEL), FOX_WIDTH),
        "g_final": gain(ks[13], (D_MODEL,)),
    }

def first_block(x, positions, e_g_in, e_w_in, e_g_q_a, e_w_q_up, e_g_kv_a, e_w_kv_up, e_sinks,
              e_w_out, o_g_in, o_w_in, o_b_f, o_w_out, g_final):
    for layer in range(DEPTH):
        j = layer // 2
        if layer % 2 == 0:
            x = mla_swa_layer(x, positions, e_g_in[j], e_w_in[j], e_g_q_a[j], e_w_q_up[j],
                              e_g_kv_a[j], e_w_kv_up[j], e_sinks[j], e_w_out[j])
        else:
            x = fox_layer(x, o_g_in[j], o_w_in[j], o_b_f[j], o_w_out[j])
    return rms_norm(x, g_final)


DEPTH_2 = 1

MIX_WIDTH = D_MODEL
MLSTM_WIDTH = D_MODEL // 2
MLSTM_HEADS = 4
MLSTM_HEAD_DIM = MLSTM_WIDTH // MLSTM_HEADS
CHUNK = 64
CONV_WIDTH = 4
POOL_WIDTH = MIX_WIDTH - MLSTM_WIDTH
POOL_WINDOWS = (2, 4, 8, 16)
POOL_GROUP = POOL_WIDTH // len(POOL_WINDOWS)
N_IN = 4 * MLSTM_WIDTH + 2 * MLSTM_HEADS + POOL_WIDTH
MEM_LEN = 256
XATTN_HEADS = 4
XATTN_HEAD_DIM = D_MODEL // XATTN_HEADS
N_EXPERTS = 16
N_GROUPS = 4
EXPERTS_PER_GROUP = N_EXPERTS // N_GROUPS
TOP_K = 2
D_EXPERT = D_MODEL // 4
MOE_BLOCK = 128
DEEPNORM_ALPHA = (2 * DEPTH_2) ** 0.25
DEEPNORM_BETA = (8 * DEPTH_2) ** -0.25
LN_EPS = 1e-5


def layer_norm(x, g, b):
    xf = x.astype(jnp.float32)
    mu = xf.mean(-1, keepdims=True)
    var = jnp.square(xf - mu).mean(-1, keepdims=True)
    return ((xf - mu) * lax.rsqrt(var + LN_EPS) * g + b).astype(x.dtype)

def causal_depthwise_conv(u, w):
    S = u.shape[1]
    K = w.shape[0]
    up = jnp.pad(u, ((0, 0), (K - 1, 0), (0, 0)))
    return sum(up[:, j:j + S] * w[j] for j in range(K))

def mlstm_chunkwise(q, k, v, i_pre, f_pre):
    B, S, H, dh = q.shape
    L = CHUNK
    NC = S // L

    def chunk(t):
        t = t.reshape((B, NC, L, H) + t.shape[3:])
        return jnp.moveaxis(t, 3, 1)

    q = chunk(q.astype(jnp.float32)) * dh ** -0.5
    k = chunk(k.astype(jnp.float32))
    v = chunk(v.astype(jnp.float32))
    ig = chunk(i_pre.astype(jnp.float32))
    b = jnp.cumsum(jax.nn.log_sigmoid(chunk(f_pre.astype(jnp.float32))), axis=-1)
    b_last = b[..., -1]

    w_state = b_last[..., None] - b + ig
    m_loc = w_state.max(-1)
    a = jnp.exp(w_state - m_loc[..., None])
    C_loc = jnp.einsum('bhcl,bhcld,bhcle->bhcde', a, k, v)
    n_loc = jnp.einsum('bhcl,bhcld->bhcd', a, k)

    def step(carry, inp):
        C, n, m = carry
        Cl, nl, ml, bl = inp
        m_new = jnp.maximum(bl + m, ml)
        s_old = jnp.exp(bl + m - m_new)
        s_new = jnp.exp(ml - m_new)
        C_new = s_old[..., None, None] * C + s_new[..., None, None] * Cl
        n_new = s_old[..., None] * n + s_new[..., None] * nl
        return (C_new, n_new, m_new), (C, n, m)

    init = (jnp.zeros((B, H, dh, dh), jnp.float32),
            jnp.zeros((B, H, dh), jnp.float32),
            jnp.zeros((B, H), jnp.float32))
    xs = tuple(jnp.moveaxis(t, 2, 0) for t in (C_loc, n_loc, m_loc, b_last))
    _, (C_prev, n_prev, m_prev) = lax.scan(step, init, xs)
    C_prev = jnp.moveaxis(C_prev, 0, 2)
    n_prev = jnp.moveaxis(n_prev, 0, 2)
    m_prev = jnp.moveaxis(m_prev, 0, 2)

    causal = jnp.tril(jnp.ones((L, L), dtype=bool))
    log_d = jnp.where(causal, b[..., :, None] - b[..., None, :] + ig[..., None, :], -jnp.inf)
    log_inter = b + m_prev[..., None]
    m_t = jnp.maximum(log_d.max(-1), log_inter)
    p = jnp.exp(log_d - m_t[..., None]) * jnp.einsum('bhcld,bhcsd->bhcls', q, k)
    inter = jnp.exp(log_inter - m_t)
    num = (jnp.einsum('bhcls,bhcse->bhcle', p, v)
           + inter[..., None] * jnp.einsum('bhcld,bhcde->bhcle', q, C_prev))
    den = p.sum(-1) + inter * jnp.einsum('bhcld,bhcd->bhcl', q, n_prev)
    h = num / jnp.maximum(jnp.abs(den), jnp.exp(-m_t))[..., None]
    return jnp.moveaxis(h, 1, 3).reshape(B, S, H, dh)

def multiscale_pool(u):
    S = u.shape[1]
    pos = jnp.arange(1, S + 1, dtype=jnp.float32)[:, None]
    outs = []
    for g, w in enumerate(POOL_WINDOWS):
        ug = u[..., g * POOL_GROUP:(g + 1) * POOL_GROUP].astype(jnp.float32)
        cs = jnp.cumsum(ug, axis=1)
        lagged = jnp.pad(cs, ((0, 0), (w, 0), (0, 0)))[:, :S]
        outs.append((cs - lagged) / jnp.minimum(pos, w) - ug)
    return jnp.stack(outs, axis=2)

def hybrid_mixer(x, w_in, b_i, b_f, conv_qk, head_norm_g, pool_w, pool_scale, w_out):
    B, S, _ = x.shape
    M, H, dh = MLSTM_WIDTH, MLSTM_HEADS, MLSTM_HEAD_DIM
    z = x @ w_in
    qk = jax.nn.silu(causal_depthwise_conv(z[..., :2 * M], conv_qk))
    q = qk[..., :M].reshape(B, S, H, dh)
    k = qk[..., M:].reshape(B, S, H, dh)
    v = z[..., 2 * M:3 * M].reshape(B, S, H, dh)
    o_pre = z[..., 3 * M:4 * M]
    i_pre = z[..., 4 * M:4 * M + H] + b_i
    f_pre = z[..., 4 * M + H:4 * M + 2 * H] + b_f
    u = z[..., 4 * M + 2 * H:]

    h = mlstm_chunkwise(q, k, v, i_pre, f_pre)
    mu = h.mean(-1, keepdims=True)
    var = jnp.square(h - mu).mean(-1, keepdims=True)
    h = (h - mu) * lax.rsqrt(var + LN_EPS) * head_norm_g.reshape(H, dh).astype(jnp.float32)
    h = h.reshape(B, S, M) * jax.nn.sigmoid(o_pre.astype(jnp.float32))

    pooled = multiscale_pool(u)
    pm = jnp.einsum('bsgc,gcd->bsgd', pooled, pool_w.astype(jnp.float32))
    pm = pm.reshape(B, S, POOL_WIDTH) * pool_scale.astype(jnp.float32)

    mixed = jnp.concatenate([h, pm], axis=-1).astype(x.dtype)
    return mixed @ w_out

def memory_cross_attention(x, mem, w_q, w_kv, w_o):
    B, S, D = x.shape
    Mlen = mem.shape[1]
    q = (x @ w_q).reshape(B, S, XATTN_HEADS, XATTN_HEAD_DIM)
    kv = (mem @ w_kv).reshape(B, Mlen, 2, XATTN_HEADS, XATTN_HEAD_DIM)
    s = jnp.einsum('bshd,bmhd->bhsm', q, kv[:, :, 0]).astype(jnp.float32) * XATTN_HEAD_DIM ** -0.5
    p = jax.nn.softmax(s, axis=-1).astype(x.dtype)
    o = jnp.einsum('bhsm,bmhd->bshd', p, kv[:, :, 1]).reshape(B, S, D)
    return o @ w_o

def grouped_moe(x, router_w, router_bias, w_gate, w_up, w_down):
    B, S, D = x.shape
    T = B * S
    A = T * TOP_K
    xt = x.reshape(T, D)
    scores = jax.nn.sigmoid((xt @ router_w).astype(jnp.float32))
    sel = scores + router_bias.astype(jnp.float32)
    grp_score = lax.top_k(sel.reshape(T, N_GROUPS, EXPERTS_PER_GROUP), 2)[0].sum(-1)
    best = jnp.argmax(grp_score, axis=-1)
    in_grp = (jnp.arange(N_EXPERTS) // EXPERTS_PER_GROUP)[None, :] == best[:, None]
    _, idx = lax.top_k(jnp.where(in_grp, sel, -jnp.inf), TOP_K)
    gate = jnp.take_along_axis(scores, idx, axis=-1)
    gate = gate / gate.sum(-1, keepdims=True)

    e = idx.reshape(A).astype(jnp.int32)
    e_sorted, order = lax.sort((e, jnp.arange(A, dtype=jnp.int32)), num_keys=1)
    counts = jnp.bincount(e, length=N_EXPERTS)
    padded = (counts + MOE_BLOCK - 1) // MOE_BLOCK * MOE_BLOCK
    pend = jnp.cumsum(padded)
    pstart = pend - padded
    start = jnp.cumsum(counts) - counts
    dest_sorted = pstart[e_sorted] + jnp.arange(A, dtype=jnp.int32) - start[e_sorted]
    R = A + N_EXPERTS * MOE_BLOCK
    NB = R // MOE_BLOCK
    buf = jnp.zeros((R, D), x.dtype).at[dest_sorted].set(xt[order // TOP_K])
    blk_e = jnp.minimum(jnp.searchsorted(pend, jnp.arange(NB, dtype=jnp.int32) * MOE_BLOCK,
                                         side='right'), N_EXPERTS - 1)

    def expert_block(args):
        xb, ei = args
        hb = jax.nn.silu(xb @ w_gate[ei]) * (xb @ w_up[ei])
        return hb @ w_down[ei]

    yb = lax.map(expert_block, (buf.reshape(NB, MOE_BLOCK, D), blk_e)).reshape(R, D)
    dest = jnp.zeros((A,), jnp.int32).at[order].set(dest_sorted)
    y = (yb[dest].reshape(T, TOP_K, D) * gate[..., None].astype(x.dtype)).sum(1)
    return y.reshape(B, S, D)

def second_inputs(seed: int = 0) -> dict:
    key = jax.random.key(seed)
    ks = jax.random.split(key, 24)
    f32 = jnp.float32
    D, L_ = D_MODEL, DEPTH_2
    beta = DEEPNORM_BETA
    nrm = lambda k, shape, s: jax.random.normal(k, shape, f32) * s
    col_scale = jnp.asarray(np.concatenate([
        np.ones(2 * MLSTM_WIDTH), np.full(MLSTM_WIDTH, beta), np.ones(MLSTM_WIDTH + 2 * MLSTM_HEADS),
        np.full(POOL_WIDTH, beta)]).astype(np.float32))
    kv_scale = jnp.asarray(np.concatenate([np.ones(D), np.full(D, beta)]).astype(np.float32))
    return {
        "x": nrm(ks[0], (BATCH, SEQ, D), 1.0),
        "mem": nrm(ks[1], (BATCH, MEM_LEN, D), 1.0),
        "w_in": nrm(ks[2], (L_, D, N_IN), D ** -0.5) * col_scale,
        "b_i": nrm(ks[3], (L_, MLSTM_HEADS), 0.1),
        "b_f": jnp.linspace(3.0, 6.0, MLSTM_HEADS, dtype=f32)[None, :] + nrm(ks[4], (L_, MLSTM_HEADS), 0.1),
        "conv_qk": nrm(ks[5], (L_, CONV_WIDTH, 2 * MLSTM_WIDTH), CONV_WIDTH ** -0.5),
        "head_norm_g": 1.0 + nrm(ks[6], (L_, MLSTM_WIDTH), 0.05),
        "pool_w": nrm(ks[7], (L_, len(POOL_WINDOWS), POOL_GROUP, POOL_GROUP), POOL_GROUP ** -0.5),
        "pool_scale": 1.0 + nrm(ks[8], (L_, POOL_WIDTH), 0.1),
        "w_mix_out": nrm(ks[9], (L_, MIX_WIDTH, D), MIX_WIDTH ** -0.5 * beta),
        "ln_mix_g": 1.0 + nrm(ks[10], (L_, D), 0.05),
        "ln_mix_b": nrm(ks[11], (L_, D), 0.02),
        "w_xq": nrm(ks[12], (L_, D, D), D ** -0.5),
        "w_xkv": nrm(ks[13], (L_, D, 2 * D), D ** -0.5) * kv_scale,
        "w_xo": nrm(ks[14], (L_, D, D), D ** -0.5 * beta),
        "ln_x_g": 1.0 + nrm(ks[15], (L_, D), 0.05),
        "ln_x_b": nrm(ks[16], (L_, D), 0.02),
        "router_w": nrm(ks[17], (D, N_EXPERTS), D ** -0.5),
        "router_bias": nrm(ks[18], (N_EXPERTS,), 0.01),
        "w_gate": nrm(ks[19], (L_, N_EXPERTS, D, D_EXPERT), D ** -0.5 * beta),
        "w_up": nrm(ks[20], (L_, N_EXPERTS, D, D_EXPERT), D ** -0.5 * beta),
        "w_down": nrm(ks[21], (L_, N_EXPERTS, D_EXPERT, D), D_EXPERT ** -0.5 * beta),
        "ln_moe_g": 1.0 + nrm(ks[22], (L_, D), 0.05),
        "ln_moe_b": nrm(ks[23], (L_, D), 0.02),
    }

def second_block(x, mem, w_in, b_i, b_f, conv_qk, head_norm_g, pool_w, pool_scale, w_mix_out,
              ln_mix_g, ln_mix_b, w_xq, w_xkv, w_xo, ln_x_g, ln_x_b, router_w, router_bias,
              w_gate, w_up, w_down, ln_moe_g, ln_moe_b):
    for l in range(DEPTH_2):
        mix = hybrid_mixer(x, w_in[l], b_i[l], b_f[l], conv_qk[l], head_norm_g[l],
                           pool_w[l], pool_scale[l], w_mix_out[l])
        x = layer_norm(DEEPNORM_ALPHA * x + mix, ln_mix_g[l], ln_mix_b[l])
        xa = memory_cross_attention(x, mem, w_xq[l], w_xkv[l], w_xo[l])
        x = layer_norm(DEEPNORM_ALPHA * x + xa, ln_x_g[l], ln_x_b[l])
        ff = grouped_moe(x, router_w, router_bias, w_gate[l], w_up[l], w_down[l])
        x = layer_norm(DEEPNORM_ALPHA * x + ff, ln_moe_g[l], ln_moe_b[l])
    return x


def setup_inputs(seed=0):
    out = dict(first_inputs(seed))
    for name, value in second_inputs(seed + 1).items():
        if name != "x":
            out[name + "_2"] = value
    return out


def reference(
    x, positions, e_g_in, e_w_in, e_g_q_a, e_w_q_up, e_g_kv_a, e_w_kv_up, e_sinks, e_w_out,
    o_g_in, o_w_in, o_b_f, o_w_out, g_final, mem_2, w_in_2, b_i_2, b_f_2, conv_qk_2,
    head_norm_g_2, pool_w_2, pool_scale_2, w_mix_out_2, ln_mix_g_2, ln_mix_b_2, w_xq_2, w_xkv_2,
    w_xo_2, ln_x_g_2, ln_x_b_2, router_w_2, router_bias_2, w_gate_2, w_up_2, w_down_2,
    ln_moe_g_2, ln_moe_b_2,
):
    x = first_block(
        x, positions, e_g_in, e_w_in, e_g_q_a, e_w_q_up, e_g_kv_a, e_w_kv_up, e_sinks, e_w_out,
        o_g_in, o_w_in, o_b_f, o_w_out, g_final,
    )
    return second_block(
        x, mem_2, w_in_2, b_i_2, b_f_2, conv_qk_2, head_norm_g_2, pool_w_2, pool_scale_2,
        w_mix_out_2, ln_mix_g_2, ln_mix_b_2, w_xq_2, w_xkv_2, w_xo_2, ln_x_g_2, ln_x_b_2,
        router_w_2, router_bias_2, w_gate_2, w_up_2, w_down_2, ln_moe_g_2, ln_moe_b_2,
    )


_drawn_inputs = setup_inputs


def setup_inputs(seed=0):
    import zlib

    import numpy as np

    out = dict(_drawn_inputs(seed))
    spreads = {}
    factors = {'e_g_in': 3.056,
     'e_g_q_a': 8.0,
     'e_g_kv_a': 8.0,
     'e_sinks': 36.514,
     'b_i_2': 64.0,
     'head_norm_g_2': 4.912,
     'router_bias_2': 2.912,
     'ln_moe_b_2': 2.853,
     'o_g_in': 8.0,
     'o_b_f': 5.364,
     'pool_scale_2': 3.677}
    for name, (base, spread) in spreads.items():
        noise = np.random.default_rng([zlib.crc32(name.encode()), seed]).standard_normal(out[name].shape)
        drawn = base * np.exp(spread * noise) if base else spread * noise
        out[name] = __import__('jax').numpy.asarray(drawn.astype(out[name].dtype))
    for name, factor in factors.items():
        out[name] = (out[name] * factor).astype(out[name].dtype)
    return out
```

```python
from contextlib import ExitStack

import concourse.bass as bass
from concourse import mybir

F32 = mybir.dt.float32
BF16 = mybir.dt.bfloat16
I32 = mybir.dt.int32
ALU = mybir.AluOpType
ACT = mybir.ActivationFunctionType
AXX = mybir.AxisListType.X
MUL, ADD, SUB, MAX, MIN = ALU.mult, ALU.add, ALU.subtract, ALU.max, ALU.min

S = 1024
D = 1024
NT = 8
NK = 8
EPS = 1e-6
LN_EPS = 1e-5
ALPHA = 2.0 ** 0.25
BIG = 1e30
PI = 3.14159274101257
TWO_PI = 6.283185307179586
C1 = 6.28125
C2 = 0.0019340515136718750
C3 = TWO_PI - C1 - C2
MAGIC = 12582912.0

C_ID = 0
C_MQ = 128
C_MT = 256
C_DM = 384
C_IC = 640
C_IF = 704
C_BD = 720
C_N = 752


class Engine:

    def __init__(self, eng, sem):
        self.eng, self.sem, self.n, self.seen = eng, sem, 0, {}

    def wait(self, *tokens):
        for sem, value in tokens:
            if self.seen.get(id(sem), 0) < value:
                self.eng.wait_ge(sem, value)
                self.seen[id(sem)] = value

    def own(self):
        self.wait((self.sem, self.n))

    def __call__(self, ins):
        ins.then_inc(self.sem, 1)
        self.n += 1
        return (self.sem, self.n)


class Slots:

    def __init__(self, bufs):
        self.bufs, self.freed, self.at = bufs, [()] * len(bufs), 0

    def take(self, *engines):
        i = self.at
        self.at = (i + 1) % len(self.bufs)
        for e in engines:
            e.wait(*self.freed[i])
        self.freed[i] = None
        return i, self.bufs[i]

    def get(self, *engines):
        while self.freed[self.at] is None:
            yield
        return self.take(*engines)

    def free(self, i, *tokens):
        self.freed[i] = tokens


class Counter:

    def __init__(self, sem):
        self.sem, self.n = sem, 0

    def __call__(self, ins):
        ins.then_inc(self.sem, 16)
        self.n += 16
        return (self.sem, self.n)


def pipeline(gens, width):
    gens = list(gens)
    live = []
    while gens or live:
        if gens and len(live) < width:
            live.append(gens.pop(0))
        done = []
        for g in live:
            if next(g, "end") == "end":
                done.append(g)
        live = [g for g in live if g not in done]
        yield


def together(*parts):
    live = [[g, pace] for g, pace in parts]
    while live:
        for p in list(live):
            for _ in range(p[1]):
                if next(p[0], "end") == "end":
                    live.remove(p)
                    break
        yield


def run(g):
    for _ in g:
        pass


def program(nc, x, positions, e_g_in, e_w_in, e_g_q_a, e_w_q_up, e_g_kv_a, e_w_kv_up, e_sinks, e_w_out,
            o_g_in, o_w_in, o_b_f, o_w_out, g_final, mem_2, w_in_2, b_i_2, b_f_2, conv_qk_2,
            head_norm_g_2, pool_w_2, pool_scale_2, w_mix_out_2, ln_mix_g_2, ln_mix_b_2, w_xq_2, w_xkv_2,
            w_xo_2, ln_x_g_2, ln_x_b_2, router_w_2, router_bias_2, w_gate_2, w_up_2, w_down_2,
            ln_moe_g_2, ln_moe_b_2, cst, out, dbg=None):
    ctx = ExitStack()
    with ctx:
        sem_names = iter(range(1000))

        def sem():
            return ctx.enter_context(nc.semaphore(f"s{next(sem_names)}"))

        A = ctx.enter_context(nc.sbuf_tensor("arena", [128, 53000], F32))
        PS = ctx.enter_context(nc.psum_tensor("banks", [128, 4096], F32))
        identb = ctx.enter_context(nc.sbuf_tensor("identb", [128, 128], BF16))
        maskq = ctx.enter_context(nc.sbuf_tensor("maskq", [128, 128], BF16))
        maskt = ctx.enter_context(nc.sbuf_tensor("maskt", [128, 128], BF16))
        posi = ctx.enter_context(nc.sbuf_tensor("posi", [128, 8], I32))
        x1 = nc.dram_tensor("x1_scratch", (S, D), F32).ap()
        x2 = nc.dram_tensor("x2_scratch", (S, D), F32).ap()
        x3 = nc.dram_tensor("x3_scratch", (S, D), F32).ap()
        x4 = nc.dram_tensor("x4_scratch", (S, D), F32).ap()

        V = Engine(nc.vector, sem())
        C = Engine(nc.scalar, sem())
        P = Engine(nc.tensor, sem())
        G = Engine(nc.gpsimd, sem())
        Y = Engine(nc.sync, sem())
        vec, act, pe, pool, sync = nc.vector, nc.scalar, nc.tensor, nc.gpsimd, nc.sync

        KW = 256
        top = [0]

        def area(words):
            a = top[0]
            top[0] += words
            assert top[0] <= 53000, top[0]
            return A[:, a:a + words]

        HT = area(32 * KW).rearrange("p (k s) -> p k s", k=8)
        OT = area(32 * KW).rearrange("p (k s) -> p k s", k=8)
        WR = [area(16 * KW) for _ in range(4)]
        XBa = [area(4 * KW) for _ in range(3)]
        SCR0 = top[0]
        SCR = area(60 * KW)
        CST = area(C_N)
        ST = area(560)
        WF = area(8 * 36).rearrange("p (k c) -> p k c", k=8)
        ident = CST[:, C_ID:C_ID + 128]

        def scr(kb, words):
            return SCR[:, int(kb * KW):int(kb * KW) + words]

        c_in = Counter(sem())
        c_w = [Counter(sem()) for _ in range(4)]
        c_x = [Counter(sem()) for _ in range(3)]
        c_m = [Counter(sem()) for _ in range(24)]
        c_sx = [Counter(sem()) for _ in range(3)]
        c_sn = [Counter(sem()) for _ in range(2)]
        m_at = [0]

        def once(*dmas):
            c = c_m[m_at[0]]
            m_at[0] += 1
            for dst, src in dmas:
                t = c(sync.dma_start(dst, src, allow_slow_non_contiguous=True))
            return t

        XB = Slots(XBa)
        W = Slots(WR)
        SB = Slots([PS[:, 0:1024], PS[:, 1024:2048]])
        TB = Slots([PS[:, 2048:2560], PS[:, 2560:3072]])
        GB = Slots([PS[:, 3072:3584], PS[:, 3584:4096]])

        def wload(parts, n_cols):
            i, buf = W.take(Y)
            for src, at in parts:
                k = src.shape[0] // 128
                view = buf[:, 0:k * n_cols].rearrange("p (k c) -> p k c", k=k)
                w = src.shape[1]
                t = c_w[i](sync.dma_start(view[:, :, at:at + w], src.rearrange("(k p) c -> p k c", p=128)))
            return i, buf[:, 0:k * n_cols].rearrange("p (k c) -> p k c", k=k), t

        def mm(o, a, b, start, stop):
            return pe.matmul(o, a, b, start=start, stop=stop)

        t_cst = once((CST, cst))
        t_pos = once((posi[:, :], positions[0].rearrange("(t p) -> p t", p=128)))
        V.wait(t_cst)
        V(vec.tensor_copy(identb[:, :], ident))
        V(vec.tensor_copy(maskq[:, :], CST[:, C_MQ:C_MQ + 128]))
        t_const = V(vec.tensor_copy(maskt[:, :], CST[:, C_MT:C_MT + 128]))
        for e in (P, C, G):
            e.wait(t_cst, t_const)

        def bcast_row(dst, row):
            return (dst, row.partition_broadcast(128))

        st_at = [0]

        def stats(n):
            a = st_at[0]
            st_at[0] += n
            assert st_at[0] <= 560
            return ST[:, a:a + n]

        def rsqrt(v, y, tmp, t_v):
            C.wait(t_v)
            t = C(act.activation(y, v, ACT.Ln))
            C.wait(t)
            t = C(act.activation(y, y, ACT.Exp, scale=-0.5))
            V.wait(t)
            V(vec.tensor_tensor(tmp, y, y, MUL))
            V.own()
            V(vec.scalar_tensor_tensor(tmp, tmp, -0.5, v, MUL, MUL))
            V.own()
            t = V(vec.scalar_tensor_tensor(y, tmp, 1.5, y, ADD, MUL))
            V.wait(t)
            return t

        def to_feature_major(src, dst, t_src, flip=0):
            toks = []
            for half in range(2):
                i, bank = yield from TB.get(P)
                P.wait(t_src)
                for j in range(4):
                    k = 4 * half + j
                    m = pe.transpose(bank[:, 128 * j:128 * j + 128], src[:, 128 * k:128 * k + 128], ident)
                t = P(m)
                view = bank.rearrange("p (k s) -> p k s", k=4)
                if half == flip:
                    C.wait(t)
                    e = C(act.activation(dst[:, 4 * half:4 * half + 4, :], view, ACT.Copy))
                else:
                    V.wait(t)
                    e = V(vec.tensor_copy(dst[:, 4 * half:4 * half + 4, :], view))
                TB.free(i, e)
                toks.append(e)
                yield
            return (t, *toks)

        XN = Slots([scr(52, 1024), scr(56, 1024)])
        ent = [stats(4) for _ in range(3)]
        ht_ready = [None] * NT

        def cols(buf, t):
            return buf[:, :, 128 * t:128 * t + 128]

        def rms_entry(t, xb, t_x, gain, t_gain, release, store=None):
            s = ent[t % 3]
            ni, xn = yield from XN.get(C, V)
            C.wait(*t_x)
            a = C(act.activation(xn, xb, ACT.Square, scale=1.0 / 32.0, accum_out=s[:, 0:1]))
            yield
            V.wait(a)
            b = V(vec.tensor_scalar(s[:, 1:2], s[:, 0:1], EPS, None, ADD))
            yield
            rsqrt(s[:, 1:2], s[:, 2:3], s[:, 3:4], b)
            V.wait(t_gain, *t_x)
            n = V(vec.scalar_tensor_tensor(xn, xb, s[:, 2:3], gain, MUL, MUL))
            release(n)
            yield
            toks = yield from to_feature_major(xn, cols(HT, t), n, t % 2)
            keep = [toks[0]]
            if store is not None:
                G.wait(n)
                keep.append(c_sn[ni](pool.dma_start(store[128 * t:128 * t + 128, :], xn)))
            XN.free(ni, *keep)
            ht_ready[t] = toks[1:]


        def stores():
            return [(c.sem, c.n) for c in (*c_sx, *c_sn)]

        def load_x(src, t, after=()):
            i, buf = XB.take(Y)
            Y.wait(*after)
            return i, buf, c_x[i](sync.dma_start(buf, src[128 * t:128 * t + 128, :]))

        GN = SCR[:, 0:1024]
        gq = SCR[:, 1024:1024 + 256]
        gkv = SCR[:, 1280:1280 + 128]
        t_g = once(bcast_row(GN, e_g_in[0]), bcast_row(gq, e_g_q_a[0]), bcast_row(gkv, e_g_kv_a[0]))
        snk = stats(8)
        t_snk = once(bcast_row(snk, e_sinks[0]))
        wi = e_w_in[0]
        wA = wload([(wi[:, 0:416], 0)], 416)
        xin = x[0]
        xload = {}
        for t in range(3):
            xload[t] = load_x(xin, t)
        iq, wqk, _ = wload([(e_w_q_up[0], 0)], 768)
        wkv = W.bufs[iq][:, 1536:1536 + 1024]
        up = e_w_kv_up[0].rearrange("p (h a c) -> a p h c", h=8, a=2)
        for a in range(2):
            t_wq = c_w[iq](sync.dma_start(wkv[:, 512 * a:512 * a + 512].rearrange("p (h c) -> p h c", h=8), up[a]))

        cosT = SCR[:, 1408:1408 + 256].rearrange("p (t c) -> p t c", t=8)
        sinT = SCR[:, 1664:1664 + 256].rearrange("p (t c) -> p t c", t=8)
        an = SCR[:, 1920:1920 + 512]
        posf = an[:, 0:8]
        ang = an[:, 16:144]
        kk = an[:, 144:272]
        ang3 = ang.rearrange("p (t c) -> p t c", t=8)
        invf = CST[:, C_IF:C_IF + 16]
        V.wait(t_pos)
        V(vec.tensor_copy(posf, posi[:, :]))
        V.own()
        for t in range(NT):
            V(vec.tensor_scalar(ang3[:, t, :], invf, posf[:, t:t + 1], None, MUL))
        V.own()
        V(vec.tensor_scalar(kk, ang, 1.0 / TWO_PI, MAGIC, MUL, ADD))
        V.own()
        V(vec.tensor_scalar(kk, kk, MAGIC, None, SUB))
        for c in (C1, C2, C3):
            V.own()
            V(vec.scalar_tensor_tensor(ang, kk, -c, ang, MUL, ADD))
        V.own()
        sa = an[:, 272:400]
        V(vec.tensor_scalar(sa, ang, -3.1415925, 3.1415925, MAX, MIN))
        V(vec.tensor_scalar(kk, ang, PI / 2, None, ADD))
        V.own()
        V(vec.tensor_scalar(ang, kk, PI, -TWO_PI, ALU.is_gt, MUL))
        V.own()
        V(vec.tensor_tensor(kk, kk, ang, ADD))
        V.own()
        t_an = V(vec.tensor_scalar(kk, kk, -3.1415925, 3.1415925, MAX, MIN))
        C.wait(t_an)
        C(act.activation(sinT[:, :, 16:32], sa.rearrange("p (t c) -> p t c", t=8), ACT.Sin))
        for h in range(2):
            t_sin = C(act.activation(cosT[:, :, 16 * h:16 * h + 16], kk.rearrange("p (t c) -> p t c", t=8), ACT.Sin))
        V.wait(t_sin)
        t_rope = V(vec.tensor_scalar(sinT[:, :, 0:16], sinT[:, :, 16:32], -1.0, None, MUL))
        V.wait(t_rope)

        def rope(dst, src, tmp, t, heads):
            co = cosT[:, t:t + 1, :].to_broadcast([128, heads, 32])
            s0 = sinT[:, t:t + 1, 0:16].to_broadcast([128, heads, 16])
            s1 = sinT[:, t:t + 1, 16:32].to_broadcast([128, heads, 16])
            V(vec.tensor_tensor(tmp[:, :, 0:16], src[:, :, 16:32], s0, MUL))
            V(vec.tensor_tensor(tmp[:, :, 16:32], src[:, :, 0:16], s1, MUL))
            V(vec.tensor_tensor(dst, src, co, MUL))
            V.own()
            return V(vec.tensor_tensor(dst, dst, tmp, ADD))

        CQT = OT[:, 6:8, :]
        CKVT = OT[:, 5, :]
        KPT = OT[0:32, 4, :]
        CN = Slots([SCR[:, 2432:2432 + 448], SCR[:, 2880:2880 + 448]])
        an2 = [stats(8) for _ in range(3)]
        lat_ready = [None] * NT

        def project_a(t):
            s = an2[t % 3]
            gi, bank = yield from GB.get(P)
            P.wait(wA[2], *ht_ready[t])
            for k in range(NK):
                m = mm(bank[:, 0:416], HT[:, k, 128 * t:128 * t + 128], wA[1][:, k, :], k == 0, k == 7)
            z = P(m)
            ci, cn = yield from CN.get(C, V)
            yield
            C.wait(z)
            C(act.activation(cn[:, 0:256], bank[:, 0:256], ACT.Square, scale=1.0 / 16.0, accum_out=s[:, 0:1]))
            a = C(act.activation(cn[:, 256:384], bank[:, 256:384], ACT.Square, scale=128.0 ** -0.5,
                                 accum_out=s[:, 1:2]))
            yield
            V.wait(a)
            b = V(vec.tensor_scalar(s[:, 2:4], s[:, 0:2], EPS, None, ADD))
            rsqrt(s[:, 2:4], s[:, 4:6], s[:, 6:8], b)
            V.wait(t_g)
            V(vec.scalar_tensor_tensor(cn[:, 0:256], bank[:, 0:256], s[:, 4:5], gq, MUL, MUL))
            V(vec.scalar_tensor_tensor(cn[:, 256:384], bank[:, 256:384], s[:, 5:6], gkv, MUL, MUL))
            r = rope(cn[:, 384:416].rearrange("p (h c) -> p h c", h=1),
                     bank[:, 384:416].rearrange("p (h c) -> p h c", h=1),
                     cn[:, 416:448].rearrange("p (h c) -> p h c", h=1), t, 1)
            GB.free(gi, r)
            yield
            ti, tb = yield from TB.get(P)
            P.wait(r)
            for j in range(3):
                pe.transpose(tb[:, 128 * j:128 * j + 128], cn[:, 128 * j:128 * j + 128], ident)
            p = P(pe.transpose(tb[0:32, 384:512], cn[:, 384:416], ident))
            CN.free(ci, p)
            yield
            V.wait(p)
            V(vec.tensor_copy(OT[:, 6:8, 128 * t:128 * t + 128], tb[:, 0:256].rearrange("p (k s) -> p k s", k=2)))
            V(vec.tensor_copy(CKVT[:, 128 * t:128 * t + 128], tb[:, 256:384]))
            e = V(vec.tensor_copy(KPT[:, 128 * t:128 * t + 128], tb[0:32, 384:512]))
            TB.free(ti, e)
            lat_ready[t] = (e,)

        def first_block_steps(t):
            i, buf, tx = xload[t]

            def release(n):
                XB.free(i, n)
                if t + 3 < NT:
                    xload[t + 3] = load_x(xin, t + 3)

            yield from rms_entry(t, buf, [tx], GN, t_g, release)
            yield
            yield from project_a(t)

        run(pipeline([first_block_steps(t) for t in range(NT)], 3))
        W.free(wA[0], (P.sem, P.n))

        w_g1 = wload([(wi[:, 1184:1696], 0)], 512)
        vi, vbuf = W.take(C, V)
        VM = vbuf.rearrange("p (t c) -> p t c", t=8)
        QT8 = scr(0, 8192).rearrange("p (h s) -> p h s", h=8)
        KA = [scr(32 + 4 * i, 1024) for i in range(4)]
        QTOK = Slots([scr(48, 1024), scr(52, 1024)])
        vm_ready = [None] * NT
        qt_ready = [None] * NT
        cs_rope = [cosT, sinT]
        ROT = scr(56, 512)
        V.own()
        V(vec.tensor_copy(ROT[:, 0:256], SCR[:, 1408:1664]))
        t_rot = V(vec.tensor_copy(ROT[:, 256:512], SCR[:, 1664:1920]))
        cosT = ROT[:, 0:256].rearrange("p (t c) -> p t c", t=8)
        sinT = ROT[:, 256:512].rearrange("p (t c) -> p t c", t=8)
        V.wait(t_rot)
        C.wait(t_rot)
        MSC = 96.0 ** -0.5

        def mla_q(t):
            si, sb2 = yield from SB.get(P)
            P.wait(t_wq, *lat_ready[t])
            for n in range(2):
                for k in range(2):
                    m = mm(sb2[:, 512 * n:512 * n + 384], CQT[:, k, 128 * t:128 * t + 128],
                           wqk[:, k, 384 * n:384 * n + 384], k == 0, k == 1)
            z = P(m)
            gi, bank = yield from GB.get(P)
            v = P(mm(bank, CKVT[:, 128 * t:128 * t + 128],
                     wkv[:, 512:1024], True, True))
            yield
            qi, qtok = yield from QTOK.get(C, V)
            C.wait(z, v)
            for n in range(2):
                a = C(act.activation(qtok[:, 384 * n:384 * n + 384], sb2[:, 512 * n:512 * n + 384], ACT.Copy,
                                     scale=MSC))
            SB.free(si, a)
            b = C(act.activation(VM[:, t, :], bank, ACT.Copy))
            GB.free(gi, b)
            vm_ready[t] = b
            yield
            V.wait(a)
            q3 = qtok[:, 0:768].rearrange("p (h c) -> p h c", h=8)[:, :, 64:96]
            tmp = qtok[:, 768:1024].rearrange("p (h c) -> p h c", h=8)
            co = cosT[:, t:t + 1, :].to_broadcast([128, 8, 32])
            s0 = sinT[:, t:t + 1, 0:16].to_broadcast([128, 8, 16])
            s1 = sinT[:, t:t + 1, 16:32].to_broadcast([128, 8, 16])
            V(vec.tensor_tensor(tmp[:, :, 0:16], q3[:, :, 16:32], s0, MUL))
            V(vec.tensor_tensor(tmp[:, :, 16:32], q3[:, :, 0:16], s1, MUL))
            V.own()
            V(vec.tensor_tensor(q3, q3, co, MUL))
            V.own()
            r = V(vec.tensor_tensor(q3, q3, tmp, ADD))
            yield
            for half in range(2):
                ti, tb = yield from TB.get(P)
                P.wait(r)
                for j in range(4):
                    h = 4 * half + j
                    m = pe.transpose(tb[0:96, 128 * j:128 * j + 128], qtok[:, 96 * h:96 * h + 96], ident)
                p = P(m)
                dst = QT8[0:96, 4 * half:4 * half + 4, 128 * t:128 * t + 128]
                E = (C, V)[half]
                E.wait(p)
                view = tb[0:96, :].rearrange("p (k s) -> p k s", k=4)
                e = C(act.activation(dst, view, ACT.Copy)) if half == 0 else V(vec.tensor_copy(dst, view))
                TB.free(ti, e)
                qt_ready[t] = (*(qt_ready[t] or ()), e)
                yield
            QTOK.free(qi, p)

        run(pipeline([mla_q(t) for t in range(NT)], 3))
        V.wait(*[q for r in qt_ready for q in r])
        for i in range(4):
            t_kpe = V(vec.tensor_copy(KA[i][64:96, :], KPT))

        PB = Slots([scr(48, 1024), scr(52, 1024)])
        PTs = Slots([scr(56, 1024)])
        for e in (C, V):
            e.wait((P.sem, P.n), (V.sem, V.n))
        OGs = Slots([stats(128) for _ in range(2)])
        GT = Slots([XBa[0], XBa[1]])
        GE = Slots([XBa[2][:, 0:256], XBa[2][:, 256:512]])
        at8 = Slots([stats(8) for _ in range(6)])
        og_bufs = OGs

        def silu_into(dst, psum, z, w):
            gi, ge = yield from GE.get(C)
            C.wait(z)
            a = C(act.activation(ge[:, 0:w], psum, ACT.Exp, scale=-1.0))
            yield
            V.wait(a)
            V(vec.tensor_scalar(ge[:, 0:w], ge[:, 0:w], 1.0, None, ADD))
            V.own()
            V(vec.reciprocal(ge[:, 0:w], ge[:, 0:w]))
            V.own()
            b = V(vec.tensor_tensor(dst, psum, ge[:, 0:w], MUL))
            GE.free(gi, b)
            return b

        def attend(q_of, k_of, v_of, t, key, need, done):
            n = 128 * (t + 1)
            si, sc = yield from SB.get(P)
            P.wait(*need)
            for b in range(0, n, 512):
                w = min(512, n - b)
                last = b + w == n
                m = mm(sc[:, b:b + w], q_of(t), k_of(b, w), True, not last)
            m = mm(sc[:, n - 128:n], identb[:, :], maskq[:, :], False, True)
            z = P(m)
            yield
            ai, s = yield from at8.get(V)
            V.wait(z)
            x1_ = V(vec.tensor_reduce(s[:, 0:1], sc[:, 0:n], AXX, MAX, negate=True))
            yield
            pi, pb = yield from PB.get(C)
            C.wait(x1_)
            e = C(act.activation(pb[:, 0:n], sc[:, 0:n], ACT.Exp, bias=s[:, 0:1], accum_out=s[:, 1:2]))
            SB.free(si, e)
            yield
            V.wait(e)
            rl = V(vec.reciprocal(s[:, 2:3], s[:, 1:2]))
            qi, pt = yield from PTs.get(V, C)
            evs = []
            for b in range(0, t + 1, 4):
                w = min(4, t + 1 - b)
                ti, tb = yield from TB.get(P)
                P.wait(e)
                for j in range(w):
                    m = pe.transpose(tb[:, 128 * j:128 * j + 128], pb[:, 128 * (b + j):128 * (b + j + 1)], ident)
                p = P(m)
                E = V if (b == 0) == (t < 4) else C
                E.wait(p)
                o, i_ = pt[:, 128 * b:128 * (b + w)], tb[:, 0:128 * w]
                ev = V(vec.tensor_copy(o, i_)) if E is V else C(act.activation(o, i_, ACT.Copy))
                TB.free(ti, ev)
                evs.append(ev)
            PB.free(pi, p)
            yield
            gi, bank = yield from GB.get(P)
            P.wait(*evs)
            for b in range(t + 1):
                m = mm(bank[:, 0:64], pt[:, 128 * b:128 * b + 128], v_of(b), b == 0, b == t)
            p = P(m)
            PTs.free(qi, p)
            yield
            f = yield from done(bank[:, 0:64], s[:, 2:3], p, rl)
            GB.free(gi, f)
            at8.free(ai, f)

        ot_ready = [None] * NT

        def finish_pair(pair, t, ogs, toks):
            oi, og = ogs
            ti, tb = yield from TB.get(P)
            P.wait(*toks)
            p = P(pe.transpose(tb[:, 0:128], og, ident))
            OGs.free(oi, p)
            yield
            C.wait(p)
            e = C(act.activation(OT[:, pair, 128 * t:128 * t + 128], tb[:, 0:128], ACT.Copy))
            TB.free(ti, e)
            ot_ready[t] = e

        def pair_attention(pair, q_of, k_of, v_of, gate, need, gate_ready):
            for t in range(NT):
                og = {}

                def head(h, t=t, og=og):
                    def done(o, rl, p, rl_t):
                        if h == 0:
                            og["slot"] = yield from OGs.get(V)
                        V.wait(p, rl_t, *gate_ready(t))
                        f = V(vec.scalar_tensor_tensor(og["slot"][1][:, 64 * h:64 * h + 64], o, rl,
                                                       gate[:, t, 64 * h:64 * h + 64], MUL, MUL))
                        og[h] = f
                        yield
                        if h == 1:
                            yield from finish_pair(pair, t, og["slot"], (og[0], og[1]))
                        return f

                    return attend(lambda t_: q_of(h, t_), lambda b, w: k_of(h, b, w),
                                  lambda b: v_of(h, b), t, h, need(h, t), done)

                for h in range(2):
                    yield head(h)

        def swap(gens_of_gens, width):
            return pipeline(gens_of_gens, width)

        kfree = {0: (), 1: (), 2: (), 3: ()}
        k_ready = {}
        g_ready = {}
        gates = {}

        def mla_prepare(p):
            gi, bank = None, None
            k_ready[p] = []
            for n in range(2):
                gi, bank = yield from GB.get(P)
                P.wait(t_wq, *lat_ready[7])
                z = P(mm(bank, wkv[:, 128 * p:128 * p + 128], CKVT[:, 512 * n:512 * n + 512], True, True))
                C.wait(z)
                for h in range(2):
                    b = 2 * (p % 2) + h
                    C.wait(*kfree[b])
                    e = C(act.activation(KA[b][0:64, 512 * n:512 * n + 512], bank[64 * h:64 * h + 64, :], ACT.Copy))
                GB.free(gi, e)
                k_ready[p].append(e)
                yield
            k_ready[p] = [*k_ready[p], t_kpe]
            yield from gate_steps(p, w_g1, 128 * p)

        def gate_steps(p, w, at):
            gt_i, gt = yield from GT.get(V)
            gt = gt.rearrange("p (t c) -> p t c", t=8)
            gates[p] = (gt_i, gt)
            g_ready[p] = [None] * NT
            for t in range(NT):
                gi, bank = yield from GB.get(P)
                P.wait(w[2], *ht_ready[t])
                for k in range(NK):
                    m = mm(bank[:, 0:128], HT[:, k, 128 * t:128 * t + 128], w[1][:, k, at:at + 128], k == 0, k == 7)
                z = P(m)
                b = yield from silu_into(gt[:, t, :], bank[:, 0:128], z, 128)
                GB.free(gi, b)
                g_ready[p][t] = b
                yield

        def mla_attend(p):
            def q_of(h, t):
                return QT8[0:96, 2 * p + h, 128 * t:128 * t + 128]

            def k_of(h, b, w):
                return KA[2 * (p % 2) + h][0:96, b:b + w]

            def v_of(h, b):
                return VM[:, b, 64 * (2 * p + h):64 * (2 * p + h) + 64]

            yield from pipeline(pair_attention(
                p, q_of, k_of, v_of, gates[p][1],
                lambda h, t: [*k_ready[p], *[q for r in qt_ready[:t + 1] for q in r], *vm_ready[:t + 1]],
                lambda t: (g_ready[p][t],)), 3)
            for h in range(2):
                kfree[2 * (p % 2) + h] = ((P.sem, P.n),)
            GT.free(gates[p][0], (V.sem, V.n))

        run(mla_prepare(0))
        w_sq = wload([(wi[:, 416:928], 0)], 512)
        for p in range(4):
            if p < 3:
                run(together((mla_attend(p), 2), (mla_prepare(p + 1), 1)))
            else:
                run(mla_attend(3))
        W.free(w_g1[0], (P.sem, P.n))
        W.free(iq, (P.sem, P.n))
        W.free(vi, (P.sem, P.n))

        w_skv = wload([(wi[:, 928:1184], 0)], 256)
        w_g2 = wload([(wi[:, 1696:2208], 0)], 512)
        P.wait((C.sem, C.n), (V.sem, V.n))
        for e in (C, V):
            e.wait((P.sem, P.n))
        KS = [scr(0, 1024), scr(4, 1024)]
        VS = scr(8, 1024).rearrange("p (t c) -> p t c", t=8)
        QS = [scr(12, 1024), scr(16, 1024)]
        SW = Slots([scr(20 + 2 * i, 512) for i in range(4)])
        PW = Slots([scr(28 + 2 * i, 512) for i in range(4)])
        ks_ready = []
        for n in range(2):
            gi, bank = GB.take(P)
            P.wait(w_skv[2])
            for k in range(NK):
                m = mm(bank, w_skv[1][:, k, 0:128], HT[:, k, 512 * n:512 * n + 512], k == 0, k == 7)
            z = P(m)
            C.wait(z)
            for g in range(2):
                for h in range(2):
                    e = C(act.activation(KS[g][64 * h:64 * h + 64, 512 * n:512 * n + 512],
                                         bank[64 * g:64 * g + 64, :], ACT.Copy))
            GB.free(gi, e)
            ks_ready.append(e)
        for t in range(NT):
            gi, bank = GB.take(P)
            for k in range(NK):
                m = mm(bank[:, 0:128], HT[:, k, 128 * t:128 * t + 128], w_skv[1][:, k, 128:256], k == 0, k == 7)
            z = P(m)
            C.wait(z)
            e = C(act.activation(VS[:, t, :], bank[:, 0:128], ACT.Copy))
            GB.free(gi, e)
        ks_ready.append(e)
        W.free(w_skv[0], (P.sem, P.n))
        qs_ready = {}
        qs_free = {0: (), 1: ()}
        DM = CST[:, C_DM:C_DM + 256]

        def swa_prepare(p):
            qs_ready[p] = []
            for n in range(2):
                gi, bank = yield from GB.get(P)
                P.wait(w_sq[2])
                for k in range(NK):
                    m = mm(bank, w_sq[1][:, k, 128 * p:128 * p + 128], HT[:, k, 512 * n:512 * n + 512],
                           k == 0, k == 7)
                z = P(m)
                C.wait(z, *qs_free[p % 2])
                e = C(act.activation(QS[p % 2][:, 512 * n:512 * n + 512], bank, ACT.Copy, scale=0.125))
                GB.free(gi, e)
                qs_ready[p].append(e)
                yield
            yield from gate_steps(4 + p, w_g2, 128 * p)

        def swa_block(p, t):
            lo = 128 if t == 0 else 0
            k0 = 128 * t - 128 + lo
            w = 256 - lo
            si, sc = yield from SB.get(P)
            P.wait(*qs_ready[p], *ks_ready)
            for h in range(2):
                m = mm(sc[:, 512 * h + lo:512 * h + 256], QS[p % 2][64 * h:64 * h + 64, 128 * t:128 * t + 128],
                       KS[p // 2][64 * h:64 * h + 64, k0:k0 + w], True, True)
            z = P(m)
            yield
            wi_, sw = yield from SW.get(V, C)
            ai, s = yield from at8.get(V)
            V.wait(z)
            sw3 = sw.rearrange("p (h c) -> p h c", h=2)
            for h in range(2):
                slope = 2.0 ** -(2 * p + h + 1)
                b = V(vec.scalar_tensor_tensor(sw3[:, h, lo:256], DM[:, lo:256], -slope,
                                               sc[:, 512 * h + lo:512 * h + 256], MUL, ADD))
            SB.free(si, b)
            V.wait(b)
            V(vec.tensor_reduce(s[:, 0:2], sw3[:, :, lo:256], AXX, MAX))
            V.own()
            V.wait(t_snk)
            V(vec.tensor_tensor(s[:, 0:2], s[:, 0:2], snk[:, 2 * p:2 * p + 2], MAX))
            V.own()
            V(vec.tensor_tensor(s[:, 2:4], snk[:, 2 * p:2 * p + 2], s[:, 0:2], SUB))
            a = V(vec.tensor_scalar(s[:, 0:2], s[:, 0:2], -1.0, None, MUL))
            yield
            pi, pw = yield from PW.get(C, V)
            C.wait(a)
            for h in range(2):
                C(act.activation(sw3[:, h, lo:256], sw3[:, h, lo:256], ACT.Exp, bias=s[:, h:h + 1],
                                 accum_out=s[:, 4 + h:5 + h]))
            e = C(act.activation(s[:, 2:4], s[:, 2:4], ACT.Exp))
            yield
            V.wait(e)
            V(vec.tensor_tensor(s[:, 4:6], s[:, 4:6], s[:, 2:4], ADD))
            V.own()
            rl = V(vec.reciprocal(s[:, 6:8], s[:, 4:6]))
            ti, tb = yield from TB.get(P)
            P.wait(e)
            blocks = [1] if t == 0 else [0, 1]
            for h in range(2):
                for c in blocks:
                    m = pe.transpose(tb[:, 256 * h + 128 * c:256 * h + 128 * c + 128],
                                     sw3[:, h, 128 * c:128 * c + 128], ident)
            p_ = P(m)
            SW.free(wi_, p_)
            C.wait(p_)
            ev = C(act.activation(pw.rearrange("p (h c) -> p h c", h=2)[:, :, lo:256],
                                  tb.rearrange("p (h c) -> p h c", h=2)[:, :, lo:256], ACT.Copy))
            TB.free(ti, ev)
            yield
            gi, bank = yield from GB.get(P)
            P.wait(ev)
            kv = p // 2
            for h in range(2):
                for c in blocks:
                    m = mm(bank[:, 64 * h:64 * h + 64], pw[:, 256 * h + 128 * c:256 * h + 128 * c + 128],
                           VS[:, t - 1 + c, 64 * kv:64 * kv + 64], c == blocks[0], c == 1)
            o = P(m)
            PW.free(pi, o)
            yield
            og = yield from OGs.get(V)
            V.wait(o, rl, g_ready[4 + p][t])
            for h in range(2):
                f = V(vec.scalar_tensor_tensor(og[1][:, 64 * h:64 * h + 64], bank[:, 64 * h:64 * h + 64],
                                               s[:, 6 + h:7 + h], gates[4 + p][1][:, t, 64 * h:64 * h + 64],
                                               MUL, MUL))
            GB.free(gi, f)
            at8.free(ai, f)
            yield
            yield from finish_pair(4 + p, t, og, (f,))

        def swa_attend(p):
            yield from pipeline((swa_block(p, t) for t in range(NT)), 3)
            qs_free[p % 2] = ((P.sem, P.n),)
            GT.free(gates[4 + p][0], (V.sem, V.n))

        run(swa_prepare(0))
        w_o = [wload([(e_w_out[0][:, 0:512], 0)], 512)]
        for p in range(4):
            if p < 3:
                run(together((swa_attend(p), 1), (swa_prepare(p + 1), 1)))
            else:
                run(swa_attend(3))
        W.free(w_sq[0], (P.sem, P.n))
        W.free(w_g2[0], (P.sem, P.n))
        w_o.append(wload([(e_w_out[0][:, 512:1024], 0)], 512))

        def all_engines_meet():
            toks = [(e.sem, e.n) for e in (P, C, V)] + [t for t in stores() if t[1]]
            for e in (P, C, V, Y, G):
                e.wait(*toks)

        def reuse_x():
            XB.freed = [()] * 3
            XB.at = 0
            XN.freed = [()] * 2
            XN.at = 0

        def project_out(t, w_o, xl):
            si, sb2 = SB.take(P)
            for n in range(2):
                P.wait(w_o[n][2])
                for k in range(NK):
                    m = mm(sb2[:, 512 * n:512 * n + 512], OT[:, k, 128 * t:128 * t + 128], w_o[n][1][:, k, :],
                           k == 0, k == 7)
            return si, sb2, P(m)

        def after_first(t, w_o, src, dst, gain, t_gain, store_norm):
            i, buf, tx = xload[t]
            si, sb2, z = project_out(t, w_o, None)
            yield
            V.wait(z, tx)
            r = V(vec.tensor_tensor(buf, buf, sb2, ADD))
            SB.free(si, r)
            keep = []
            if dst is not None:
                G.wait(r)
                keep.append(c_sx[i](pool.dma_start(dst[128 * t:128 * t + 128, :], buf)))

            def release(n):
                XB.free(i, n, *keep)
                if t + 3 < NT:
                    xload[t + 3] = load_x(src, t + 3)

            yield
            yield from rms_entry(t, buf, [r], gain, t_gain, release, store_norm)

        all_engines_meet()
        reuse_x()
        GN = scr(48, 1024)
        t_g = once(bcast_row(GN, o_g_in[0]))
        for t in range(3):
            xload[t] = load_x(xin, t)
        run(pipeline([after_first(t, w_o, xin, x1, GN, t_g, None) for t in range(NT)], 3))
        for w in w_o:
            W.free(w[0], (P.sem, P.n))
        x1_done = stores()

        all_engines_meet()
        wo_ = o_w_in[0]
        t_wf = once((WF[:, :, 0:16], wo_[:, 3072:3088].rearrange("(k p) c -> p k c", p=128)))
        bfc = stats(1)
        t_bf = once((bfc[0:16, :], o_b_f[0].rearrange("(p a) -> p a", a=1)))

        def fox_weights(p):
            return wload([(wo_[:, 128 * p:128 * p + 128], 0), (wo_[:, 1024 + 128 * p:1152 + 128 * p], 128),
                          (wo_[:, 2048 + 128 * p:2176 + 128 * p], 256),
                          (wo_[:, 3088 + 128 * p:3216 + 128 * p], 384)], 512)

        fw = {p: fox_weights(p) for p in range(3)}
        QA = [scr(4 * i, 1024) for i in range(4)]
        KA = [scr(16 + 4 * i, 1024) for i in range(4)]
        VG = [scr(32 + 8 * i, 2048).rearrange("p (t c) -> p t c", t=8) for i in range(2)]
        PB = Slots([scr(48, 1024), scr(52, 1024)])
        PTs = Slots([scr(56, 1024)])
        GE = Slots([XBa[2][:, 0:256], XBa[2][:, 256:512]])
        LC = XBa[0]
        NLC = XBa[1]

        def log_sigmoid(x_, e_, n):
            V(vec.scalar_tensor_tensor(e_, x_, -1.0, x_, MUL, MAX))
            C.wait((V.sem, V.n))
            C(act.activation(e_, e_, ACT.Exp, scale=-1.0))
            C.own()
            a = C(act.activation(e_, e_, ACT.Ln, bias=1.0))
            V.wait(a)
            return V(vec.scalar_tensor_tensor(x_, x_, 0.0, e_, MIN, SUB))

        for n in range(2):
            gi, bank = GB.take(P)
            P.wait(t_wf, *[q for r in ht_ready for q in r])
            for k in range(NK):
                m = mm(bank[0:16, :], WF[:, k, 0:16], HT[:, k, 512 * n:512 * n + 512], k == 0, k == 7)
            z = P(m)
            V.wait(z, t_bf)
            e = V(vec.tensor_scalar(LC[0:16, 512 * n:512 * n + 512], bank[0:16, :], bfc[0:16, :], None, ADD))
            GB.free(gi, e)
        V.own()
        log_sigmoid(LC[0:16, :], NLC[0:16, :], 1024)
        zz = XBa[2][0:16, :]
        V(vec.memset(zz, 1.0))
        V.own()
        t_c = V(vec.tensor_tensor_scan(LC[0:16, :], zz, LC[0:16, :], 0.0, MUL, ADD))
        V.own()
        t_nc = V(vec.tensor_scalar(NLC[0:16, :], LC[0:16, :], -1.0, None, MUL))
        for i in range(4):
            V(vec.memset(QA[i][64:66, :], 1.0))
            t_ones = V(vec.memset(KA[i][64:66, :], 1.0))
        C.wait(t_nc)
        Y.wait(t_nc, t_ones)
        c_aug = [Counter(sem()) for _ in range(4)]
        qkfree = {0: (), 1: ()}
        vg_free = {0: (), 1: ()}
        fq_ready, fv_ready, faug = {}, {}, {}

        def fox_prepare(p):
            w = fw[p]
            par = p % 2
            Y.wait(*qkfree[par])
            faug[p] = []
            for h in range(2):
                b = 2 * par + h
                c_aug[b](sync.dma_start(QA[b][64:65, :], LC[2 * p + h:2 * p + h + 1, :]))
                faug[p].append(c_aug[b](sync.dma_start(KA[b][65:66, :], NLC[2 * p + h:2 * p + h + 1, :])))
            fq_ready[p] = []
            for which, bufs, scale in ((0, QA, 0.125), (1, KA, 1.0)):
                for n in range(2):
                    gi, bank = yield from GB.get(P)
                    P.wait(w[2])
                    for k in range(NK):
                        m = mm(bank, w[1][:, k, 128 * which:128 * which + 128], HT[:, k, 512 * n:512 * n + 512],
                               k == 0, k == 7)
                        if k == 3:
                            yield
                    z = P(m)
                    C.wait(z, *qkfree[par])
                    for h in range(2):
                        e = C(act.activation(bufs[2 * par + h][0:64, 512 * n:512 * n + 512],
                                             bank[64 * h:64 * h + 64, :], ACT.Copy, scale=scale))
                    GB.free(gi, e)
                    fq_ready[p].append(e)
                    yield
            fv_ready[p] = [None] * NT
            for t in range(NT):
                gi, bank = yield from GB.get(P)
                for k in range(NK):
                    m = mm(bank[:, 0:256], HT[:, k, 128 * t:128 * t + 128], w[1][:, k, 256:512], k == 0, k == 7)
                    if k == 3:
                        yield
                z = P(m)
                C.wait(z, *vg_free[par])
                V.wait(*vg_free[par])
                C(act.activation(VG[par][:, t, 0:128], bank[:, 0:128], ACT.Copy))
                a = (C.sem, C.n)
                b = yield from silu_into(VG[par][:, t, 128:256], bank[:, 128:256], z, 128)
                GB.free(gi, b, a)
                fv_ready[p][t] = (a, b)
                yield
            W.free(w[0], (P.sem, P.n))
            if p + 3 < 8:
                fw[p + 3] = fox_weights(p + 3)

        def fox_attend(p):
            par = p % 2

            def q_of(h, t):
                return QA[2 * par + h][0:66, 128 * t:128 * t + 128]

            def k_of(h, b, w):
                return KA[2 * par + h][0:66, b:b + w]

            def v_of(h, b):
                return VG[par][:, b, 64 * h:64 * h + 64]

            yield from pipeline(pair_attention(
                p, q_of, k_of, v_of, VG[par][:, :, 128:256],
                lambda h, t: [*faug[p], *fq_ready[p], *[r[0] for r in fv_ready[p][:t + 1]]],
                lambda t: (fv_ready[p][t][1],)), 3)
            qkfree[par] = ((P.sem, P.n),)
            vg_free[par] = ((P.sem, P.n), (V.sem, V.n))

        run(fox_prepare(0))
        for p in range(8):
            if p < 7:
                run(together((fox_attend(p), 1), (fox_prepare(p + 1), 1)))
            else:
                w_o = [wload([(o_w_out[0][:, 512 * n:512 * n + 512], 0)], 512) for n in range(2)]
                run(fox_attend(p))

        all_engines_meet()
        reuse_x()
        GN = scr(48, 1024)
        t_g = once(bcast_row(GN, g_final))
        Y.wait(*x1_done)
        for t in range(3):
            xload[t] = load_x(x1, t)
        run(pipeline([after_first(t, w_o, x1, None, GN, t_g, x2) for t in range(NT)], 3))
        for w in w_o:
            W.free(w[0], (P.sem, P.n))
        x2_done = stores()

        all_engines_meet()
        wm = w_in_2[0]
        V(vec.memset(WF[:, :, :], 0.0))
        Y.wait((V.sem, V.n))
        t_wf = once((WF[:, :, 0:4], wm[:, 2048:2052].rearrange("(k p) c -> p k c", p=128)),
                    (WF[:, :, 32:36], wm[:, 2052:2056].rearrange("(k p) c -> p k c", p=128)))
        bic = stats(2)
        CW = stats(32).rearrange("p (k j) -> p k j", k=8)
        PSC = stats(4)
        t_small = once((bic[0:4, 0:1], b_i_2[0].rearrange("(p a) -> p a", a=1)),
                       (bic[0:4, 1:2], b_f_2[0].rearrange("(p a) -> p a", a=1)),
                       (PSC, pool_scale_2[0].rearrange("(g p) -> p g", p=128)),
                       *[(CW[:, :, j], conv_qk_2[0][j].rearrange("(k p) -> p k", p=128)) for j in range(4)])

        def mix_weights(h):
            return wload([(wm[:, 512 * j + 128 * h:512 * j + 128 * h + 128], 128 * j) for j in range(4)], 512)

        mw = {h: mix_weights(h) for h in range(3)}
        ZB = scr(0, 1028)
        CV = [scr(4.5, 1024), scr(8.5, 1024)]
        EX = scr(12.5, 1024)
        VO = scr(16.5, 8 * 260).rearrange("p (t c) -> p t c", t=8)
        KTm = scr(25, 1024).rearrange("p (t c) -> p t c", t=8)
        GR = scr(29, 1024)
        GC = scr(33, 1024).rearrange("p (t c) -> p t c", t=8)
        WB = scr(37, 1024)
        T0 = scr(41, 1024)
        T1 = scr(45, 1024)
        HG = scr(49, 512)
        EM = Slots([scr(51, 128), scr(51.5, 128), scr(52, 128)])
        CS = scr(52.5, 132)
        NUM = Slots([scr(53.5, 132), scr(54.5, 132)])
        HN = Slots([scr(55.5, 128), scr(56, 128)])
        SOb = scr(56.5, 32)
        SO4 = scr(57, 32)
        MP = scr(57.25, 8)
        SO = scr(57.5, 8)
        SEL = scr(58, 512)
        t_hg = once(bcast_row(HG, head_norm_g_2[0]))

        for n in range(2):
            gi, bank = GB.take(P)
            P.wait(t_wf)
            for k in range(NK):
                m = mm(bank[0:36, :], WF[:, k, :], HT[:, k, 512 * n:512 * n + 512], k == 0, k == 7)
            z = P(m)
            V.wait(z, t_small)
            V(vec.tensor_scalar(T0[0:4, 512 * n:512 * n + 512], bank[0:4, :], bic[0:4, 0:1], None, ADD))
            e = V(vec.tensor_scalar(T1[0:4, 512 * n:512 * n + 512], bank[32:36, :], bic[0:4, 1:2], None, ADD))
            GB.free(gi, e)
        V.own()
        IG, LF = T0[0:4, :], T1[0:4, :]
        log_sigmoid(LF, EX[0:4, :], 1024)
        m_row = CV[0][0:4, :]
        b_row = CV[1][0:4, :]
        ones_r = ZB[0:4, 0:1024]
        V(vec.memset(GR, 0.0))
        V(vec.memset(ones_r, 1.0))
        V.own()
        V(vec.memset(ones_r.rearrange("p (t c) -> p t c", t=8)[:, :, 0:1], 0.0))
        V(vec.tensor_tensor_scan(m_row, LF, IG, 0.0, ADD, MAX))
        V.own()
        V(vec.tensor_tensor_scan(b_row, ones_r, LF, 0.0, MUL, ADD))
        V(vec.memset(MP[0:4, 0:1], 0.0))
        m3 = m_row.rearrange("p (t c) -> p t c", t=8)
        b3 = b_row.rearrange("p (t c) -> p t c", t=8)
        V(vec.tensor_copy(MP[0:4, 1:8], m3[:, 0:7, 127]))
        V.own()

        def g3(a):
            return GR[a:a + 4, :].rearrange("p (t c) -> p t c", t=8)

        def rep(v):
            return v.to_broadcast([4, 8, 128])

        mp3 = MP[0:4, :].rearrange("p (t c) -> p t c", c=1)
        V(vec.tensor_tensor(g3(0), IG.rearrange("p (t c) -> p t c", t=8), b3, SUB))
        V(vec.tensor_tensor(WB[0:4, :], b_row, m_row, SUB))
        V(vec.tensor_scalar(GR[64:68, :], m_row, -1.0, None, MUL))
        V.own()
        V(vec.tensor_tensor(g3(32), WB[0:4, :].rearrange("p (t c) -> p t c", t=8), rep(mp3), ADD))
        V(vec.tensor_tensor(SO[0:4, :], b3[:, :, 127], m3[:, :, 127], SUB))
        V.own()
        so3 = SO[0:4, :].rearrange("p (t c) -> p t c", c=1)
        V(vec.tensor_tensor(g3(96), g3(0), rep(so3), ADD))
        V.own()
        V(vec.tensor_tensor(SO[0:4, :], SO[0:4, :], MP[0:4, :], ADD))
        V.own()
        C.wait((V.sem, V.n))
        e = C(act.activation(SO[0:4, :], SO[0:4, :], ACT.Exp))
        V.wait(e)
        so_b = SO[0:4, :].rearrange("p (h c) -> p h c", h=1).to_broadcast([4, 4, 8])
        V(vec.tensor_tensor(SO4[0:4, :].rearrange("p (h c) -> p h c", h=4), so_b,
                            CST[0:4, C_BD:C_BD + 32].rearrange("p (h c) -> p h c", h=4), MUL))
        V(vec.memset(SEL[0:4, :], 0.0))
        V.own()
        V(vec.tensor_copy(SEL[0:4, :].rearrange("p (h c) -> p h c", h=4),
                          CST[0:4, C_BD:C_BD + 32].rearrange("p (h c) -> p h c", h=4)[:, :, 0:1]
                          .to_broadcast([4, 4, 128])))
        V(vec.memset(ones_r[:, 0:128], 1.0))
        t_rows = (V.sem, V.n)
        P.wait(t_rows)
        gi, bank = GB.take(P)
        z = P(mm(bank[:, 0:32], ones_r[:, 0:128], SO4[0:4, :], True, True))
        V.wait(z)
        e = V(vec.tensor_copy(SOb, bank[:, 0:32]))
        GB.free(gi, e)
        for half in range(2):
            ti, tb = TB.take(P)
            for j in range(4):
                t = 4 * half + j
                m = pe.transpose(tb[:, 128 * j:128 * j + 128], GR[:, 128 * t:128 * t + 128], ident)
            z = P(m)
            tv = tb.rearrange("p (t c) -> p t c", t=4)
            V.wait(z)
            V(vec.tensor_copy(GC[:, 4 * half:4 * half + 4, 0:4], tv[:, :, 0:4]))
            C.wait((V.sem, V.n))
            e = C(act.activation(GC[:, 4 * half:4 * half + 4, 32:128], tv[:, :, 32:128], ACT.Exp))
            TB.free(ti, e)
        t_gc = e
        V.wait(e)
        V(vec.memset(ZB[:, 0:3], 0.0))
        V(vec.memset(VO[:, :, 128:129], 1.0))
        V.own()
        C.wait((V.sem, V.n))
        SCALE_M = 128.0 ** -0.5
        hst = [stats(16) for _ in range(2)]

        def mix_head(h):
            w = mw[h]
            for which in range(2):
                ch = 4 * which + h
                V.wait((P.sem, P.n))
                for n in range(2):
                    gi, bank = yield from GB.get(P)
                    P.wait(w[2])
                    for k in range(NK):
                        m = mm(bank, w[1][:, k, 128 * which:128 * which + 128], HT[:, k, 512 * n:512 * n + 512],
                               k == 0, k == 7)
                    z = P(m)
                    C.wait(z, (V.sem, V.n))
                    e = C(act.activation(ZB[:, 3 + 512 * n:515 + 512 * n], bank, ACT.Copy))
                    GB.free(gi, e)
                V.wait(e)
                cv = CV[which]
                V(vec.tensor_scalar(cv, ZB[:, 0:1024], CW[:, ch, 0:1], None, MUL))
                for j in range(1, 4):
                    V.own()
                    V(vec.scalar_tensor_tensor(cv, ZB[:, j:j + 1024], CW[:, ch, j:j + 1], cv, MUL, ADD))
                C.wait((V.sem, V.n))
                e = C(act.activation(EX, cv, ACT.Exp, scale=-1.0))
                V.wait(e)
                V(vec.tensor_scalar(EX, EX, 1.0, None, ADD))
                V.own()
                V(vec.reciprocal(EX, EX))
                V.own()
                t_qk = V(vec.tensor_tensor(cv, cv, EX, MUL))
                V.own()
            for t in range(NT):
                gi, bank = yield from GB.get(P)
                for k in range(NK):
                    m = mm(bank[:, 0:256], HT[:, k, 128 * t:128 * t + 128], w[1][:, k, 256:512], k == 0, k == 7)
                z = P(m)
                C.wait(z)
                C(act.activation(VO[:, t, 0:128], bank[:, 0:128], ACT.Copy))
                e = C(act.activation(VO[:, t, 130:258], bank[:, 128:256], ACT.Exp, scale=-1.0))
                GB.free(gi, e)
                V.wait(e)
                V(vec.tensor_scalar(VO[:, t, 130:258], VO[:, t, 130:258], 1.0, None, ADD))
                V.own()
                t_vo = V(vec.reciprocal(VO[:, t, 130:258], VO[:, t, 130:258]))
            for n in range(2):
                gi, bank = yield from GB.get(P)
                z = P(mm(bank, SEL[0:4, 128 * h:128 * h + 128], WROW[0:4, 512 * n:512 * n + 512], True, True))
                V.wait(z)
                e = V(vec.tensor_copy(WBC[:, 512 * n:512 * n + 512], bank))
                GB.free(gi, e)
            P.wait(t_qk, t_vo)
            V.own()
            for half in range(2):
                ti, tb = yield from TB.get(P)
                for j in range(4):
                    t = 4 * half + j
                    m = pe.transpose(tb[:, 128 * j:128 * j + 128], CV[1][:, 128 * t:128 * t + 128], ident)
                z = P(m)
                V.wait(z)
                for j in range(4):
                    t = 4 * half + j
                    e = V(vec.tensor_scalar(KTm[:, t, :], tb[:, 128 * j:128 * j + 128],
                                            GC[:, t, 96 + h:97 + h], None, MUL))
                TB.free(ti, e)
            P.wait(e)
            V(vec.memset(CS, 0.0))
            t_cs = (V.sem, V.n)

            def chunk(t):
                nonlocal t_cs
                ei, em = yield from EM.get(V, C)
                V.own()
                a = V(vec.tensor_tensor(em, WBC[:, 128 * t:128 * t + 128], CST[:, C_MT:C_MT + 128], ADD))
                C.wait(a)
                e = C(act.activation(em, em, ACT.Exp, bias=GC[:, t, h:h + 1]))
                si, sc = yield from SB.get(P)
                z = P(mm(sc[:, 0:128], CV[1][:, 128 * t:128 * t + 128], CV[0][:, 128 * t:128 * t + 128], True, True))
                V.wait(z, e)
                a = V(vec.scalar_tensor_tensor(em, sc[:, 0:128], SCALE_M, em, MUL, MUL))
                SB.free(si, a)
                gi, bank = yield from GB.get(P)
                P.wait(a)
                z1 = P(mm(bank[:, 0:129], em, VO[:, t, 0:129], True, True))
                EM.free(ei, z1)
                si, sc = yield from SB.get(P)
                P.wait(t_cs)
                mm(sc[:, 0:129], CV[0][:, 128 * t:128 * t + 128], CS[:, 0:129], True, True)
                z2 = P(mm(sc[:, 512:512 + 129], KTm[:, t, :], VO[:, t, 0:129], True, True))
                ni, num = yield from NUM.get(V)
                V.wait(z1, z2)
                s = hst[t % 2]
                V(vec.tensor_scalar(num[:, 0:129], sc[:, 0:129], GC[:, t, 32 + h:33 + h], SCALE_M, MUL, MUL))
                a = V(vec.scalar_tensor_tensor(CS[:, 0:129], CS[:, 0:129], SOb[:, 8 * h + t:8 * h + t + 1],
                                               sc[:, 512:512 + 129], MUL, ADD))
                t_cs = a
                SB.free(si, a)
                V.own()
                a = V(vec.tensor_tensor(num[:, 0:129], num[:, 0:129], bank[:, 0:129], ADD))
                GB.free(gi, a)
                V.own()
                V(vec.scalar_tensor_tensor(s[:, 0:1], num[:, 128:129], -1.0, num[:, 128:129], MUL, MAX))
                V.own()
                V(vec.tensor_tensor(s[:, 0:1], s[:, 0:1], GC[:, t, 64 + h:65 + h], MAX))
                V.own()
                V(vec.reciprocal(s[:, 0:1], s[:, 0:1]))
                V.own()
                V(vec.tensor_scalar(num[:, 0:128], num[:, 0:128], s[:, 0:1], None, MUL))
                V.own()
                V(vec.bn_stats(s[:, 1:7], num[:, 0:128]))
                V.own()
                V(vec.bn_aggr(s[:, 8:10], s[:, 1:7]))
                V.own()
                b = V(vec.tensor_scalar(s[:, 10:11], s[:, 9:10], LN_EPS, None, ADD))
                rsqrt(s[:, 10:11], s[:, 11:12], s[:, 12:13], b)
                V(vec.tensor_scalar(num[:, 0:128], num[:, 0:128], s[:, 8:9], s[:, 11:12], SUB, MUL))
                V.own()
                V.wait(t_hg)
                V(vec.tensor_tensor(num[:, 0:128], num[:, 0:128], HG[:, 128 * h:128 * h + 128], MUL))
                V.own()
                hi, hn = yield from HN.get(V)
                a = V(vec.tensor_tensor(hn, num[:, 0:128], VO[:, t, 130:258], MUL))
                NUM.free(ni, a)
                ti, tb = yield from TB.get(P)
                P.wait(a)
                z = P(pe.transpose(tb[:, 0:128], hn, ident))
                HN.free(hi, z)
                C.wait(z)
                e = C(act.activation(OT[:, h, 128 * t:128 * t + 128], tb[:, 0:128], ACT.Copy))
                TB.free(ti, e)
                yield

            for t in range(NT):
                yield from chunk(t)
            P.wait((C.sem, C.n), (V.sem, V.n))
            V.wait((P.sem, P.n))
            C.wait((P.sem, P.n), (V.sem, V.n))
            W.free(w[0], (P.sem, P.n))
            if h + 3 < 5:
                mw[h + 3] = mix_weights(3) if h + 3 == 3 else wload([(wm[:, 2056:2568], 0)], 512)

        WROW = T0
        V(vec.tensor_copy(T0[0:4, :], WB[0:4, :]))
        V.own()
        P.wait((V.sem, V.n))
        WBC = WB
        for h in range(4):
            run(mix_head(h))

        wi_p, wp, t_wp = mw[4]
        ip, pw_, t_pw = wload([(pool_w_2[0].rearrange("g c d -> (g c) d"), 0)], 128)
        w_o = [wload([(w_mix_out_2[0][:, 512 * n:512 * n + 512], 0)], 512) for n in range(2)]
        UB = [CV[0], CV[1]]
        for g in range(4):
            for n in range(2):
                gi, bank = GB.take(P)
                P.wait(t_wp)
                for k in range(NK):
                    m = mm(bank, wp[:, k, 128 * g:128 * g + 128], HT[:, k, 512 * n:512 * n + 512], k == 0, k == 7)
                z = P(m)
                C.wait(z, (V.sem, V.n))
                e = C(act.activation(CV[0][:, 512 * n:512 * n + 512], bank, ACT.Copy))
                GB.free(gi, e)
            V.wait(e)
            cur, nxt = CV[0], T0
            u = CV[0]
            bufs = [T0, T1]
            win = 2 ** (g + 1)
            sh = 1
            bi = 0
            while sh < win:
                o = bufs[bi]
                V(vec.tensor_copy(o[:, 0:sh], cur[:, 0:sh]))
                V(vec.tensor_tensor(o[:, sh:1024], cur[:, sh:1024], cur[:, 0:1024 - sh], ADD))
                V.own()
                cur = o
                bi ^= 1
                sh *= 2
            V.wait((P.sem, P.n))
            V(vec.tensor_tensor(cur[:, 0:16], cur[:, 0:16], CST[:, C_IC + 16 * g:C_IC + 16 * g + 16], MUL))
            V.own()
            pb_ = CV[1]
            V(vec.tensor_tensor(pb_[:, 0:16], cur[:, 0:16], u[:, 0:16], SUB))
            e = V(vec.scalar_tensor_tensor(pb_[:, 16:1024], cur[:, 16:1024], 1.0 / win, u[:, 16:1024], MUL, SUB))
            V.own()
            for n in range(2):
                gi, bank = GB.take(P)
                P.wait(t_pw, e)
                z = P(mm(bank, pw_[:, g, :], pb_[:, 512 * n:512 * n + 512], True, True))
                V.wait(z)
                f = V(vec.tensor_scalar(OT[:, 4 + g, 512 * n:512 * n + 512], bank, PSC[:, g:g + 1], None, MUL))
                GB.free(gi, f)
        W.free(wi_p, (P.sem, P.n))
        W.free(ip, (P.sem, P.n))

        lnst = [stats(18) for _ in range(3)]

        def layer_norm(t, yb, t_y, gb, bb, t_gb, xn):
            s = lnst[t % 3]
            V.wait(t_y)
            for h in range(2):
                V(vec.bn_stats(s[:, 6 * h:6 * h + 6], yb[:, 512 * h:512 * h + 512]))
            V.own()
            V(vec.bn_aggr(s[:, 12:14], s[:, 0:12]))
            V.own()
            b = V(vec.tensor_scalar(s[:, 14:15], s[:, 13:14], LN_EPS, None, ADD))
            yield
            rsqrt(s[:, 14:15], s[:, 15:16], s[:, 16:17], b)
            V(vec.tensor_scalar(xn, yb, s[:, 12:13], s[:, 15:16], SUB, MUL))
            V.own()
            V.wait(t_gb)
            V(vec.tensor_tensor(xn, xn, gb, MUL))
            V.own()
            return V(vec.tensor_tensor(xn, xn, bb, ADD))

        def after_ln(t, w_o, src, dst, gb, bb, t_gb):
            i, buf, tx = xload[t]
            si, sb2, z = project_out(t, w_o, None)
            yield
            V.wait(z, tx)
            r = V(vec.scalar_tensor_tensor(buf, buf, ALPHA, sb2, MUL, ADD))
            SB.free(si, r)
            ni, xn = yield from XN.get(V)
            n = yield from layer_norm(t, buf, r, gb, bb, t_gb, xn)
            XB.free(i, n)
            if t + 3 < NT:
                xload[t + 3] = load_x(src, t + 3)
            yield
            toks = yield from to_feature_major(xn, cols(HT, t), n, t % 2)
            G.wait(n)
            st = c_sn[ni](pool.dma_start(dst[128 * t:128 * t + 128, :], xn))
            XN.free(ni, toks[0], st)
            ht_ready[t] = toks[1:]

        all_engines_meet()
        reuse_x()
        GN, BN = scr(44, 1024), scr(48, 1024)
        t_g = once(bcast_row(GN, ln_mix_g_2[0]), bcast_row(BN, ln_mix_b_2[0]))
        Y.wait(*x2_done)
        for t in range(3):
            xload[t] = load_x(x2, t)
        run(pipeline([after_ln(t, w_o, x2, x3, GN, BN, t_g) for t in range(NT)], 3))
        for w in w_o:
            W.free(w[0], (P.sem, P.n))
        x1_done = stores()

        all_engines_meet()
        MEM = scr(0, 2048).rearrange("p (t c) -> p t c", t=2)
        MT = scr(8, 2048).rearrange("p (k s) -> p k s", k=8)
        KX = scr(16, 2048).rearrange("p (k s) -> p k s", k=8)
        VX = scr(24, 2048).rearrange("p (t c) -> p t c", t=2)
        t_mem = once((MEM, mem_2[0].rearrange("(t p) c -> p t c", p=128)))
        wx = [wload([(w_xkv_2[0][:, 512 * j:512 * j + 512], 0)], 512) for j in range(3)]
        for t in range(2):
            run_ = to_feature_major(MEM[:, t, :], MT[:, :, 128 * t:128 * t + 128], t_mem, t)
            run(run_)
        P.wait((C.sem, C.n), (V.sem, V.n))
        for j in range(2):
            for c in range(4):
                gi, bank = GB.take(P)
                P.wait(wx[j][2])
                for k in range(NK):
                    m = mm(bank[:, 0:256], wx[j][1][:, k, 128 * c:128 * c + 128], MT[:, k, :], k == 0, k == 7)
                z = P(m)
                C.wait(z)
                e = C(act.activation(KX[:, 4 * j + c, :], bank[:, 0:256], ACT.Copy))
                GB.free(gi, e)
            W.free(wx[j][0], (P.sem, P.n))
            if j == 0:
                wx.append(wload([(w_xkv_2[0][:, 1536:2048], 0)], 512))
        for j in range(2):
            for t in range(2):
                gi, bank = GB.take(P)
                P.wait(wx[2 + j][2])
                for k in range(NK):
                    m = mm(bank, MT[:, k, 128 * t:128 * t + 128], wx[2 + j][1][:, k, :], k == 0, k == 7)
                z = P(m)
                V.wait(z)
                e2 = V(vec.tensor_copy(VX[:, t, 512 * j:512 * j + 512], bank))
                GB.free(gi, e2)
            W.free(wx[2 + j][0], (P.sem, P.n))
        t_kvx = (e, e2)
        wq = [wload([(w_xq_2[0][:, 512 * j:512 * j + 512], 0)], 512) for j in range(2)]
        w_o = [wload([(w_xo_2[0][:, 512 * j:512 * j + 512], 0)], 512) for j in range(2)]
        q_ready = []
        for j in range(2):
            for c in range(4):
                for n in range(2):
                    gi, bank = GB.take(P)
                    P.wait(wq[j][2])
                    for k in range(NK):
                        m = mm(bank, wq[j][1][:, k, 128 * c:128 * c + 128], HT[:, k, 512 * n:512 * n + 512],
                               k == 0, k == 7)
                    z = P(m)
                    C.wait(z)
                    e = C(act.activation(OT[:, 4 * j + c, 512 * n:512 * n + 512], bank, ACT.Copy, scale=1.0 / 16.0))
                    GB.free(gi, e)
            W.free(wq[j][0], (P.sem, P.n))
        P.wait(*t_kvx, e)
        PX = Slots([scr(32, 1024), scr(36, 1024)])
        PXT = Slots([scr(40, 1024), scr(44, 1024)])
        OX = Slots([scr(48, 1024), XBa[0]])

        def cross(t):
            si, sc = yield from SB.get(P)
            for h in range(4):
                for k in range(2):
                    m = mm(sc[:, 256 * h:256 * h + 256], OT[:, 2 * h + k, 128 * t:128 * t + 128],
                           KX[:, 2 * h + k, :], k == 0, k == 1)
            z = P(m)
            yield
            V.wait(z)
            s = ent8[t % 3]
            a = V(vec.tensor_reduce(s[:, 0:4], sc.rearrange("p (h c) -> p h c", h=4), AXX, MAX, negate=True))
            yield
            pi, px = yield from PX.get(C)
            C.wait(a)
            for h in range(4):
                e = C(act.activation(px[:, 256 * h:256 * h + 256], sc[:, 256 * h:256 * h + 256], ACT.Exp,
                                     bias=s[:, h:h + 1], accum_out=s[:, 4 + h:5 + h]))
            SB.free(si, e)
            yield
            V.wait(e)
            rl = V(vec.reciprocal(s[:, 8:12], s[:, 4:8]))
            ti_, pxt = yield from PXT.get(C, V)
            toks = yield from to_feature_major(px, pxt.rearrange("p (k s) -> p k s", k=8), e, t % 2)
            PX.free(pi, toks[0])
            oi, ox = yield from OX.get(V)
            for h2 in range(2):
                gi, bank = yield from GB.get(P)
                P.wait(*toks)
                for h in (2 * h2, 2 * h2 + 1):
                    for k in range(2):
                        m = mm(bank[:, 256 * (h % 2):256 * (h % 2) + 256], pxt[:, 256 * h + 128 * k:256 * h + 128 * k + 128],
                               VX[:, k, 256 * h:256 * h + 256], k == 0, k == 1)
                p = P(m)
                V.wait(p)
                for h in (2 * h2, 2 * h2 + 1):
                    f = V(vec.tensor_scalar(ox[:, 256 * h:256 * h + 256], bank[:, 256 * (h % 2):256 * (h % 2) + 256],
                                            s[:, 8 + h:9 + h], None, MUL))
                GB.free(gi, f)
                yield
            PXT.free(ti_, p)
            toks = yield from to_feature_major(ox, cols(OT, t), f, t % 2)
            OX.free(oi, toks[0])
            ot_ready[t] = toks[1:]

        ent8 = [stats(12) for _ in range(3)]
        run(pipeline([cross(t) for t in range(NT)], 3))
        all_engines_meet()
        reuse_x()
        GN, BN = scr(44, 1024), scr(48, 1024)
        t_g = once(bcast_row(GN, ln_x_g_2[0]), bcast_row(BN, ln_x_b_2[0]))
        Y.wait(*x1_done)
        for t in range(3):
            xload[t] = load_x(x3, t)
        run(pipeline([after_ln(t, w_o, x3, x4, GN, BN, t_g) for t in range(NT)], 3))
        for w in w_o:
            W.free(w[0], (P.sem, P.n))
        x2_done = stores()

        all_engines_meet()
        RW = scr(0, 128).rearrange("p (k c) -> p k c", k=8)
        RBs = scr(0.5, 16)
        t_r = once((RW, router_w_2.rearrange("(k p) c -> p k c", p=128)), bcast_row(RBs, router_bias_2))
        gi, bank = GB.take(P)
        P.wait(t_r)
        for t in range(NT):
            for k in range(NK):
                m = mm(bank[:, 16 * t:16 * t + 16], HT[:, k, 128 * t:128 * t + 128], RW[:, k, :], k == 0, k == 7)
        z = P(m)
        r_at = [1]

        def rt(n=32):
            a = SCR[:, 256 * r_at[0]:256 * r_at[0] + n]
            r_at[0] += 1 if n > 128 else 0.5
            r_at[0] = int(r_at[0] + 0.5)
            return a

        SCO, SEL_, GWt, CH = rt(128), rt(128), rt(128), rt(128)
        C.wait(z)
        e = C(act.activation(SCO, bank[:, 0:128], ACT.Exp, scale=-1.0))
        GB.free(gi, e)
        V.wait(e, t_r)
        V(vec.tensor_scalar(SCO, SCO, 1.0, None, ADD))
        V.own()
        V(vec.reciprocal(SCO, SCO))
        V.own()

        def v3(a, c):
            return a.rearrange("p (t c) -> p t c", c=c)

        V(vec.tensor_tensor(v3(SEL_, 16), v3(SCO, 16), RBs.rearrange("p (a c) -> p a c", a=1).to_broadcast([128, 8, 16]), ADD))
        V.own()
        sv = v3(SEL_, 4)

        def lane(a, i):
            return v3(a, 4)[:, :, i]

        M1, N1, M2, N2, TT = [rt(32) for _ in range(5)]
        V(vec.tensor_tensor(M1, sv[:, :, 0], sv[:, :, 1], MAX))
        V(vec.tensor_tensor(N1, sv[:, :, 0], sv[:, :, 1], MIN))
        V(vec.tensor_tensor(M2, sv[:, :, 2], sv[:, :, 3], MAX))
        V(vec.tensor_tensor(N2, sv[:, :, 2], sv[:, :, 3], MIN))
        V.own()
        V(vec.tensor_tensor(TT, M1, M2, MIN))
        V(vec.tensor_tensor(N1, N1, N2, MAX))
        V(vec.tensor_tensor(M1, M1, M2, MAX))
        V.own()
        V(vec.tensor_tensor(TT, TT, N1, MAX))
        V.own()
        V(vec.tensor_tensor(TT, M1, TT, ADD))
        V.own()
        GM, FR = rt(8), rt(8)
        V(vec.tensor_reduce(GM, v3(TT, 4), AXX, MAX))
        V.own()
        EQ, IGr = rt(32), rt(32)
        V(vec.tensor_tensor(v3(EQ, 4), v3(TT, 4), GM.rearrange("p (t c) -> p t c", c=1).to_broadcast([128, 8, 4]),
                            ALU.is_equal))
        V(vec.memset(FR, 1.0))
        V.own()
        for g in range(4):
            V(vec.tensor_tensor(lane(IGr, g), lane(EQ, g), FR, MUL))
            V.own()
            V(vec.tensor_tensor(FR, FR, lane(IGr, g), SUB))
            V.own()
        RK, CM = rt(32), rt(32)
        for i in range(4):
            first = True
            for j in range(4):
                if j == i:
                    continue
                o = RK if first else CM
                V(vec.tensor_tensor(o, sv[:, :, j], sv[:, :, i], ALU.is_ge if j < i else ALU.is_gt))
                V.own()
                if not first:
                    V(vec.tensor_tensor(RK, RK, CM, ADD))
                    V.own()
                first = False
            V(vec.scalar_tensor_tensor(v3(CH, 4)[:, :, i], RK, 1.5, IGr, ALU.is_lt, MUL))
            V.own()
        V(vec.tensor_tensor(GWt, SCO, CH, MUL))
        V.own()
        V(vec.tensor_reduce(GM, v3(GWt, 16), AXX, ADD))
        V.own()
        V(vec.reciprocal(GM, GM))
        V.own()
        V(vec.tensor_tensor(v3(GWt, 16), v3(GWt, 16), GM.rearrange("p (t c) -> p t c", c=1).to_broadcast([128, 8, 16]),
                            MUL))
        V.own()
        assert r_at[0] <= 24
        gw3 = v3(GWt, 16)

        WDb = [scr(24, 2048), scr(32, 2048)]
        WD = Slots(WDb)
        c_d = [Counter(sem()), Counter(sem())]
        HS = Slots([scr(40 + 2 * i, 512) for i in range(2)])
        HTs = Slots([scr(44 + i, 256) for i in range(4)])

        def expert_weights(e_):
            w = wload([(w_gate_2[0][e_], 0), (w_up_2[0][e_], 256)], 512)
            i, buf = WD.take(Y)
            d = buf.rearrange("p (k c) -> p k c", k=2)
            t = c_d[i](sync.dma_start(d, w_down_2[0][e_].rearrange("(k p) c -> p k c", p=128)))
            return w, (i, d, t)

        ew = {e_: expert_weights(e_) for e_ in range(2)}
        for t in range(NT):
            V(vec.memset(OT[:, t, :], 0.0))
        y_last = [(V.sem, V.n)] * NT

        def expert_block(e_, t):
            w, wd = ew[e_]
            gi, bank = yield from GB.get(P)
            P.wait(w[2])
            for k in range(NK):
                m = mm(bank, HT[:, k, 128 * t:128 * t + 128], w[1][:, k, :], k == 0, k == 7)
            z = P(m)
            if t == NT - 1:
                W.free(w[0], z)
            yield
            hi, hs = yield from HS.get(C, V)
            C.wait(z)
            a = C(act.activation(hs[:, 256:512], bank[:, 0:256], ACT.Exp, scale=-1.0))
            yield
            V.wait(a)
            V(vec.tensor_scalar(hs[:, 256:512], hs[:, 256:512], 1.0, None, ADD))
            V.own()
            V(vec.reciprocal(hs[:, 256:512], hs[:, 256:512]))
            V.own()
            V(vec.scalar_tensor_tensor(hs[:, 0:256], hs[:, 256:512], gw3[:, t, e_:e_ + 1], bank[:, 0:256], MUL, MUL))
            V.own()
            b = V(vec.tensor_tensor(hs[:, 0:256], hs[:, 0:256], bank[:, 256:512], MUL))
            GB.free(gi, b)
            yield
            ti, tb = yield from TB.get(P)
            P.wait(b)
            for k in range(2):
                m = pe.transpose(tb[:, 128 * k:128 * k + 128], hs[:, 128 * k:128 * k + 128], ident)
            p = P(m)
            HS.free(hi, p)
            hti, ht = yield from HTs.get(C)
            C.wait(p)
            c = C(act.activation(ht, tb[:, 0:256], ACT.Copy))
            TB.free(ti, c)
            yield
            si, sb2 = yield from SB.get(P)
            P.wait(c, wd[2])
            for n in range(2):
                for k in range(2):
                    m = mm(sb2[:, 512 * n:512 * n + 512], ht[:, 128 * k:128 * k + 128],
                           wd[1][:, k, 512 * n:512 * n + 512], k == 0, k == 1)
            p = P(m)
            HTs.free(hti, p)
            if t == NT - 1:
                WD.free(wd[0], p)
                if e_ + 2 < 16:
                    ew[e_ + 2] = expert_weights(e_ + 2)
            yield
            V.wait(p, y_last[t])
            y_last[t] = V(vec.tensor_tensor(OT[:, t, :], OT[:, t, :], sb2, ADD))
            SB.free(si, y_last[t])

        run(pipeline((expert_block(e_, t) for e_ in range(16) for t in range(NT)), 4))

        all_engines_meet()
        reuse_x()
        GN, BN = scr(44, 1024), scr(48, 1024)
        t_g = once(bcast_row(GN, ln_moe_g_2[0]), bcast_row(BN, ln_moe_b_2[0]))
        Y.wait(*x2_done)
        for t in range(3):
            xload[t] = load_x(x4, t)

        def last(t):
            i, buf, tx = xload[t]
            V.wait(tx, y_last[t])
            r = V(vec.scalar_tensor_tensor(buf, buf, ALPHA, OT[:, t, :], MUL, ADD))
            ni, xn = yield from XN.get(V)
            n = yield from layer_norm(t, buf, r, GN, BN, t_g, xn)
            XB.free(i, n)
            if t + 3 < NT:
                xload[t + 3] = load_x(x4, t + 3)
            G.wait(n)
            st = c_sn[ni](pool.dma_start(out[0][128 * t:128 * t + 128, :], xn))
            XN.free(ni, st)
            yield

        run(pipeline([last(t) for t in range(NT)], 3))
        G.wait(*stores())


_INS = ['x', 'positions', 'e_g_in', 'e_w_in', 'e_g_q_a', 'e_w_q_up', 'e_g_kv_a', 'e_w_kv_up', 'e_sinks', 'e_w_out',
        'o_g_in', 'o_w_in', 'o_b_f', 'o_w_out', 'g_final', 'mem_2', 'w_in_2', 'b_i_2', 'b_f_2', 'conv_qk_2',
        'head_norm_g_2', 'pool_w_2', 'pool_scale_2', 'w_mix_out_2', 'ln_mix_g_2', 'ln_mix_b_2', 'w_xq_2', 'w_xkv_2',
        'w_xo_2', 'ln_x_g_2', 'ln_x_b_2', 'router_w_2', 'router_bias_2', 'w_gate_2', 'w_up_2', 'w_down_2',
        'ln_moe_g_2', 'ln_moe_b_2']


def constants():
    import numpy as np

    c = np.zeros((128, C_N), np.float32)
    c[:, C_ID:C_ID + 128] = np.eye(128)
    q = np.arange(128)
    c[:, C_MQ:C_MQ + 128] = np.where(q[None, :] > q[:, None], -BIG, 0.0)
    c[:, C_MT:C_MT + 128] = np.where(q[:, None] > q[None, :], -BIG, 0.0)
    k = np.arange(256)
    dist = 128 + q[:, None] - k[None, :]
    c[:, C_DM:C_DM + 256] = np.where((dist >= 0) & (dist < 128), dist, BIG)
    for g in range(4):
        c[:, C_IC + 16 * g:C_IC + 16 * g + 16] = 1.0 / np.minimum(np.arange(1, 17), 2 ** (g + 1))
    c[:, C_IF:C_IF + 16] = (1.0 / (np.float32(10000.0) ** (np.arange(0, 32, 2, dtype=np.float32) / np.float32(32))))
    for h in range(4):
        c[h, C_BD + 8 * h:C_BD + 8 * h + 8] = 1.0
    return c


def kernel(**inputs):
    import numpy as _np
    import concourse.bacc as _bacc
    from concourse import mybir as _mybir
    from concourse.bass_utils import run_bass_kernel_spmd as _run

    nc = _bacc.Bacc("TRN2", target_bir_lowering=False, num_devices=1)
    arrays, args = {}, []
    for name in _INS:
        a = _np.ascontiguousarray(inputs[name])
        arrays[f"in_{name}_dram"] = a
        args.append(nc.dram_tensor(f"in_{name}_dram", a.shape, _mybir.dt.from_np(a.dtype), kind="ExternalInput").ap())
    a = constants()
    arrays["in_tables_dram"] = a
    args.append(nc.dram_tensor("in_tables_dram", a.shape, _mybir.dt.from_np(a.dtype), kind="ExternalInput").ap())
    args.append(nc.dram_tensor("out_0_dram", (1, S, D), F32, kind="ExternalOutput").ap())
    program(nc, *args)
    r = _run(nc, [arrays], core_ids=[0])
    return r.results[0]["out_0_dram"]
```

```python
from contextlib import ExitStack

import concourse.bass as bass
from concourse import mybir

F32 = mybir.dt.float32
BF16 = mybir.dt.bfloat16
I32 = mybir.dt.int32
ALU = mybir.AluOpType
ACT = mybir.ActivationFunctionType
AXX = mybir.AxisListType.X
MUL, ADD, SUB, MAX, MIN = ALU.mult, ALU.add, ALU.subtract, ALU.max, ALU.min

S = 1024
D = 1024
NT = 8
NK = 8
EPS = 1e-6
LN_EPS = 1e-5
ALPHA = 2.0 ** 0.25
BIG = 1e30
PI = 3.14159274101257
TWO_PI = 6.283185307179586
C1 = 6.28125
C2 = 0.0019340515136718750
C3 = TWO_PI - C1 - C2
MAGIC = 12582912.0

C_ID = 0
C_MQ = 128
C_MT = 256
C_DM = 384
C_IC = 640
C_IF = 704
C_BD = 720
C_TR = 752
C_EB = 880
C_TI = 896
C_N = 904
CAP = 256
LIMIT = 256
NSLOT = 16 * CAP


class Engine:

    def __init__(self, eng, sem):
        self.eng, self.sem, self.n, self.seen = eng, sem, 0, {}

    def wait(self, *tokens):
        for sem, value in tokens:
            if self.seen.get(id(sem), 0) < value:
                self.eng.wait_ge(sem, value)
                self.seen[id(sem)] = value

    def own(self):
        self.wait((self.sem, self.n))

    def __call__(self, ins):
        ins.then_inc(self.sem, 1)
        self.n += 1
        return (self.sem, self.n)


class Slots:

    def __init__(self, bufs):
        self.bufs, self.freed, self.at = bufs, [()] * len(bufs), 0

    def take(self, *engines):
        i = self.at
        self.at = (i + 1) % len(self.bufs)
        for e in engines:
            e.wait(*self.freed[i])
        self.freed[i] = None
        return i, self.bufs[i]

    def get(self, *engines):
        while self.freed[self.at] is None:
            yield
        return self.take(*engines)

    def free(self, i, *tokens):
        self.freed[i] = tokens


class Counter:

    def __init__(self, sem):
        self.sem, self.n = sem, 0

    def __call__(self, ins):
        ins.then_inc(self.sem, 16)
        self.n += 16
        return (self.sem, self.n)


def pipeline(gens, width):
    gens = list(gens)
    live = []
    idle = 0
    while gens or live:
        idle += 1
        assert idle < 100000
        if gens and len(live) < width:
            live.append(gens.pop(0))
        done = []
        for g in live:
            if next(g, "end") == "end":
                done.append(g)
        live = [g for g in live if g not in done]
        yield


def together(*parts):
    live = [[g, pace] for g, pace in parts]
    while live:
        for p in list(live):
            for _ in range(p[1]):
                if next(p[0], "end") == "end":
                    live.remove(p)
                    break
        yield


def run(g):
    for _ in g:
        pass


def program(nc, x, positions, e_g_in, e_w_in, e_g_q_a, e_w_q_up, e_g_kv_a, e_w_kv_up, e_sinks, e_w_out,
            o_g_in, o_w_in, o_b_f, o_w_out, g_final, mem_2, w_in_2, b_i_2, b_f_2, conv_qk_2,
            head_norm_g_2, pool_w_2, pool_scale_2, w_mix_out_2, ln_mix_g_2, ln_mix_b_2, w_xq_2, w_xkv_2,
            w_xo_2, ln_x_g_2, ln_x_b_2, router_w_2, router_bias_2, w_gate_2, w_up_2, w_down_2,
            ln_moe_g_2, ln_moe_b_2, cst, out):
    ctx = ExitStack()
    with ctx:
        sem_names = iter(range(1000))

        def sem():
            return ctx.enter_context(nc.semaphore(f"s{next(sem_names)}"))

        A = ctx.enter_context(nc.sbuf_tensor("arena", [128, 52920], F32))
        PS = ctx.enter_context(nc.psum_tensor("banks", [128, 4096], F32))
        identb = ctx.enter_context(nc.sbuf_tensor("identb", [128, 128], BF16))
        maskq = ctx.enter_context(nc.sbuf_tensor("maskq", [128, 128], BF16))
        maskt = ctx.enter_context(nc.sbuf_tensor("maskt", [128, 128], BF16))
        IDX = ctx.enter_context(nc.sbuf_tensor("slots", [128, 32], I32))
        DI = ctx.enter_context(nc.sbuf_tensor("places", [128, 16], I32))
        FLG = ctx.enter_context(nc.sbuf_tensor("flag", [128, 1], I32))
        posi = ctx.enter_context(nc.sbuf_tensor("posi", [128, 8], I32))
        x1 = nc.dram_tensor("x1_scratch", (S, D), F32).ap()
        x2 = nc.dram_tensor("x2_scratch", (S, D), F32).ap()
        x3 = nc.dram_tensor("x3_scratch", (S, D), F32).ap()
        x4 = nc.dram_tensor("x4_scratch", (S, D), F32).ap()
        slot_out = nc.dram_tensor("slot_out", (NSLOT, D), F32).ap()

        V = Engine(nc.vector, sem())
        C = Engine(nc.scalar, sem())
        P = Engine(nc.tensor, sem())
        G = Engine(nc.gpsimd, sem())
        Y = Engine(nc.sync, sem())
        vec, act, pe, pool, sync = nc.vector, nc.scalar, nc.tensor, nc.gpsimd, nc.sync

        KW = 256
        top = [0]

        def area(words):
            words = int(words)
            a = top[0]
            top[0] += words
            assert top[0] <= 52920, top[0]
            return A[:, a:a + words]

        HT = area(32 * KW).rearrange("p (k s) -> p k s", k=8)
        OT = area(32 * KW).rearrange("p (k s) -> p k s", k=8)
        WR = [area(16 * KW) for _ in range(4)]
        XBa = [area(4 * KW) for _ in range(3)]
        SCR0 = top[0]
        SCR = area(60 * KW)
        CST = area(C_N)
        ST = area(528)
        WF = area(8 * 36).rearrange("p (k c) -> p k c", k=8)
        ident = CST[:, C_ID:C_ID + 128]

        def scr(kb, words):
            return SCR[:, int(kb * KW):int(kb * KW) + words]

        c_in = Counter(sem())
        c_w = [Counter(sem()) for _ in range(4)]
        c_x = [Counter(sem()) for _ in range(3)]
        c_m = [Counter(sem()) for _ in range(28)]
        c_sx = [Counter(sem()) for _ in range(3)]
        c_sn = [Counter(sem()) for _ in range(2)]
        m_at = [0]

        def once(*dmas):
            c = c_m[m_at[0]]
            m_at[0] += 1
            for dst, src in dmas:
                t = c(sync.dma_start(dst, src, allow_slow_non_contiguous=True))
            return t

        XB = Slots(XBa)
        W = Slots(WR)
        SB = Slots([PS[:, 0:1024], PS[:, 1024:2048]])
        TB = Slots([PS[:, 2048:2560], PS[:, 2560:3072]])
        GB = Slots([PS[:, 3072:3584], PS[:, 3584:4096]])

        def wload(parts, n_cols):
            i, buf = W.take(Y)
            for src, at in parts:
                k = src.shape[0] // 128
                view = buf[:, 0:k * n_cols].rearrange("p (k c) -> p k c", k=k)
                w = src.shape[1]
                t = c_w[i](sync.dma_start(view[:, :, at:at + w], src.rearrange("(k p) c -> p k c", p=128)))
            return i, buf[:, 0:k * n_cols].rearrange("p (k c) -> p k c", k=k), t

        def mm(o, a, b, start, stop):
            return pe.matmul(o, a, b, start=start, stop=stop)

        def tr(o, a, i):
            return pe.transpose(o, a, i)

        t_cst = once((CST, cst[:, 0:C_N]))
        t_pos = once((posi[:, :], positions[0].rearrange("(t p) -> p t", p=128)))
        V.wait(t_cst)
        V(vec.tensor_copy(identb[:, :], ident))
        V(vec.tensor_copy(maskq[:, :], CST[:, C_MQ:C_MQ + 128]))
        t_const = V(vec.tensor_copy(maskt[:, :], CST[:, C_MT:C_MT + 128]))
        for e in (P, C, G):
            e.wait(t_cst, t_const)

        def bcast_row(dst, row):
            return (dst, row.partition_broadcast(128))

        st_at = [0]

        def stats(n):
            a = st_at[0]
            st_at[0] += n
            assert st_at[0] <= 528
            return ST[:, a:a + n]

        mhalf = stats(2)
        t_mh = V(vec.memset(mhalf, -0.5))
        G.wait(t_mh)

        def rsqrt(v, y, t_v):
            G.wait(t_v)
            t = G(pool.tensor_tensor(y, v, mhalf[:, 0:v.shape[1]], ALU.pow))
            V.wait(t)
            return t

        def to_feature_major(src, dst, t_src, flip=0):
            toks = []
            for half in range(2):
                i, bank = yield from TB.get(P)
                P.wait(t_src)
                for j in range(4):
                    k = 4 * half + j
                    m = tr(bank[:, 128 * j:128 * j + 128], src[:, 128 * k:128 * k + 128], ident)
                t = P(m)
                view = bank.rearrange("p (k s) -> p k s", k=4)
                if half == flip:
                    C.wait(t)
                    e = C(act.activation(dst[:, 4 * half:4 * half + 4, :], view, ACT.Copy))
                else:
                    V.wait(t)
                    e = V(vec.tensor_copy(dst[:, 4 * half:4 * half + 4, :], view))
                TB.free(i, e)
                toks.append(e)
                yield
            return (t, *toks)

        XN = Slots([scr(52, 1024), scr(56, 1024)])
        ent = [stats(4) for _ in range(3)]
        ht_ready = [None] * NT

        def cols(buf, t):
            return buf[:, :, 128 * t:128 * t + 128]

        def rms_entry(t, xb, t_x, gain, t_gain, release, store=None):
            s = ent[t % 3]
            ni, xn = yield from XN.get(C, V)
            C.wait(*t_x)
            a = C(act.activation(xn, xb, ACT.Square, scale=1.0 / 32.0, accum_out=s[:, 0:1]))
            yield
            V.wait(a)
            b = V(vec.tensor_scalar(s[:, 1:2], s[:, 0:1], EPS, None, ADD))
            yield
            rsqrt(s[:, 1:2], s[:, 2:3], b)
            V.wait(t_gain, *t_x)
            n = V(vec.scalar_tensor_tensor(xn, xb, s[:, 2:3], gain, MUL, MUL))
            release(n)
            yield
            toks = yield from to_feature_major(xn, cols(HT, t), n, t % 2)
            keep = [toks[0]]
            if store is not None:
                Y.wait(n)
                keep.append(c_sn[ni](sync.dma_start(store[128 * t:128 * t + 128, :], xn)))
            XN.free(ni, *keep)
            ht_ready[t] = toks[1:]


        def stores():
            return [(c.sem, c.n) for c in (*c_sx, *c_sn)]

        def load_x(src, t, after=()):
            i, buf = XB.take(Y)
            Y.wait(*after)
            return i, buf, c_x[i](sync.dma_start(buf, src[128 * t:128 * t + 128, :]))

        GN = SCR[:, 0:1024]
        gq = SCR[:, 1024:1024 + 256]
        gkv = SCR[:, 1280:1280 + 128]
        t_g = once(bcast_row(GN, e_g_in[0]), bcast_row(gq, e_g_q_a[0]), bcast_row(gkv, e_g_kv_a[0]))
        snk = stats(8)
        t_snk = once(bcast_row(snk, e_sinks[0]))
        wi = e_w_in[0]
        wA = wload([(wi[:, 0:416], 0)], 416)
        xin = x[0]
        xload = {}
        for t in range(3):
            xload[t] = load_x(xin, t)
        iq, wqk, _ = wload([(e_w_q_up[0], 0)], 768)
        wkv = W.bufs[iq][:, 1536:1536 + 1024]
        up = e_w_kv_up[0].rearrange("p (h a c) -> a p h c", h=8, a=2)
        for a in range(2):
            t_wq = c_w[iq](sync.dma_start(wkv[:, 512 * a:512 * a + 512].rearrange("p (h c) -> p h c", h=8), up[a]))

        cosT = SCR[:, 1408:1408 + 256].rearrange("p (t c) -> p t c", t=8)
        sinT = SCR[:, 1664:1664 + 256].rearrange("p (t c) -> p t c", t=8)
        an = SCR[:, 1920:1920 + 512]
        posf = an[:, 0:8]
        ang = an[:, 16:144]
        kk = an[:, 144:272]
        ang3 = ang.rearrange("p (t c) -> p t c", t=8)
        invf = CST[:, C_IF:C_IF + 16]
        V.wait(t_pos)
        V(vec.tensor_copy(posf, posi[:, :]))
        V.own()
        for t in range(NT):
            V(vec.tensor_scalar(ang3[:, t, :], invf, posf[:, t:t + 1], None, MUL))
        V.own()
        V(vec.tensor_scalar(kk, ang, 1.0 / TWO_PI, MAGIC, MUL, ADD))
        V.own()
        V(vec.tensor_scalar(kk, kk, MAGIC, None, SUB))
        for c in (C1, C2, C3):
            V.own()
            V(vec.scalar_tensor_tensor(ang, kk, -c, ang, MUL, ADD))
        V.own()
        sa = an[:, 272:400]
        V(vec.tensor_scalar(sa, ang, -3.1415925, 3.1415925, MAX, MIN))
        V(vec.tensor_scalar(kk, ang, PI / 2, None, ADD))
        V.own()
        V(vec.tensor_scalar(ang, kk, PI, -TWO_PI, ALU.is_gt, MUL))
        V.own()
        V(vec.tensor_tensor(kk, kk, ang, ADD))
        V.own()
        t_an = V(vec.tensor_scalar(kk, kk, -3.1415925, 3.1415925, MAX, MIN))
        C.wait(t_an)
        C(act.activation(sinT[:, :, 16:32], sa.rearrange("p (t c) -> p t c", t=8), ACT.Sin))
        for h in range(2):
            t_sin = C(act.activation(cosT[:, :, 16 * h:16 * h + 16], kk.rearrange("p (t c) -> p t c", t=8), ACT.Sin))
        V.wait(t_sin)
        t_rope = V(vec.tensor_scalar(sinT[:, :, 0:16], sinT[:, :, 16:32], -1.0, None, MUL))
        V.wait(t_rope)

        def rope(dst, src, tmp, t, heads):
            co = cosT[:, t:t + 1, :].to_broadcast([128, heads, 32])
            s0 = sinT[:, t:t + 1, 0:16].to_broadcast([128, heads, 16])
            s1 = sinT[:, t:t + 1, 16:32].to_broadcast([128, heads, 16])
            V(vec.tensor_tensor(tmp[:, :, 0:16], src[:, :, 16:32], s0, MUL))
            V(vec.tensor_tensor(tmp[:, :, 16:32], src[:, :, 0:16], s1, MUL))
            V(vec.tensor_tensor(dst, src, co, MUL))
            V.own()
            return V(vec.tensor_tensor(dst, dst, tmp, ADD))

        CQT = OT[:, 6:8, :]
        CKVT = OT[:, 5, :]
        KPT = OT[0:32, 4, :]
        CN = Slots([SCR[:, 2432:2432 + 448], SCR[:, 2880:2880 + 448]])
        an2 = [stats(8) for _ in range(3)]
        lat_ready = [None] * NT

        def project_a(t):
            s = an2[t % 3]
            gi, bank = yield from GB.get(P)
            P.wait(wA[2], *ht_ready[t])
            for k in range(NK):
                m = mm(bank[:, 0:416], HT[:, k, 128 * t:128 * t + 128], wA[1][:, k, :], k == 0, k == 7)
            z = P(m)
            ci, cn = yield from CN.get(C, V)
            yield
            C.wait(z)
            C(act.activation(cn[:, 0:256], bank[:, 0:256], ACT.Square, scale=1.0 / 16.0, accum_out=s[:, 0:1]))
            a = C(act.activation(cn[:, 256:384], bank[:, 256:384], ACT.Square, scale=128.0 ** -0.5,
                                 accum_out=s[:, 1:2]))
            yield
            V.wait(a)
            b = V(vec.tensor_scalar(s[:, 2:4], s[:, 0:2], EPS, None, ADD))
            rsqrt(s[:, 2:4], s[:, 4:6], b)
            V.wait(t_g)
            V(vec.scalar_tensor_tensor(cn[:, 0:256], bank[:, 0:256], s[:, 4:5], gq, MUL, MUL))
            V(vec.scalar_tensor_tensor(cn[:, 256:384], bank[:, 256:384], s[:, 5:6], gkv, MUL, MUL))
            r = rope(cn[:, 384:416].rearrange("p (h c) -> p h c", h=1),
                     bank[:, 384:416].rearrange("p (h c) -> p h c", h=1),
                     cn[:, 416:448].rearrange("p (h c) -> p h c", h=1), t, 1)
            GB.free(gi, r)
            yield
            ti, tb = yield from TB.get(P)
            P.wait(r)
            for j in range(3):
                tr(tb[:, 128 * j:128 * j + 128], cn[:, 128 * j:128 * j + 128], ident)
            p = P(tr(tb[0:32, 384:512], cn[:, 384:416], ident))
            CN.free(ci, p)
            yield
            V.wait(p)
            V(vec.tensor_copy(OT[:, 6:8, 128 * t:128 * t + 128], tb[:, 0:256].rearrange("p (k s) -> p k s", k=2)))
            V(vec.tensor_copy(CKVT[:, 128 * t:128 * t + 128], tb[:, 256:384]))
            e = V(vec.tensor_copy(KPT[:, 128 * t:128 * t + 128], tb[0:32, 384:512]))
            TB.free(ti, e)
            lat_ready[t] = (e,)

        def first_block_steps(t):
            i, buf, tx = xload[t]

            def release(n):
                XB.free(i, n)
                if t + 3 < NT:
                    xload[t + 3] = load_x(xin, t + 3)

            yield from rms_entry(t, buf, [tx], GN, t_g, release)
            yield
            yield from project_a(t)

        run(pipeline([first_block_steps(t) for t in range(NT)], 4))
        W.free(wA[0], (P.sem, P.n))

        w_g1 = wload([(wi[:, 1184:1696], 0)], 512)
        vi, vbuf = W.take(C, V)
        VM = vbuf.rearrange("p (t c) -> p t c", t=8)
        QT8 = scr(0, 8192).rearrange("p (h s) -> p h s", h=8)
        KA = [scr(32 + 4 * i, 1024) for i in range(4)]
        QTOK = Slots([scr(48, 1024), scr(52, 1024)])
        vm_ready = [None] * NT
        qt_ready = [None] * NT
        cs_rope = [cosT, sinT]
        ROT = scr(56, 512)
        V.own()
        V(vec.tensor_copy(ROT[:, 0:256], SCR[:, 1408:1664]))
        t_rot = V(vec.tensor_copy(ROT[:, 256:512], SCR[:, 1664:1920]))
        cosT = ROT[:, 0:256].rearrange("p (t c) -> p t c", t=8)
        sinT = ROT[:, 256:512].rearrange("p (t c) -> p t c", t=8)
        V.wait(t_rot)
        C.wait(t_rot)
        MSC = 96.0 ** -0.5

        def mla_q(t):
            si, sb2 = yield from SB.get(P)
            P.wait(t_wq, *lat_ready[t])
            for n in range(2):
                for k in range(2):
                    m = mm(sb2[:, 512 * n:512 * n + 384], CQT[:, k, 128 * t:128 * t + 128],
                           wqk[:, k, 384 * n:384 * n + 384], k == 0, k == 1)
            z = P(m)
            gi, bank = yield from GB.get(P)
            v = P(mm(bank, CKVT[:, 128 * t:128 * t + 128],
                     wkv[:, 512:1024], True, True))
            yield
            qi, qtok = yield from QTOK.get(C, V)
            C.wait(z, v)
            for n in range(2):
                a = C(act.activation(qtok[:, 384 * n:384 * n + 384], sb2[:, 512 * n:512 * n + 384], ACT.Copy,
                                     scale=MSC))
            SB.free(si, a)
            b = C(act.activation(VM[:, t, :], bank, ACT.Copy))
            GB.free(gi, b)
            vm_ready[t] = b
            yield
            V.wait(a)
            q3 = qtok[:, 0:768].rearrange("p (h c) -> p h c", h=8)[:, :, 64:96]
            tmp = qtok[:, 768:1024].rearrange("p (h c) -> p h c", h=8)
            co = cosT[:, t:t + 1, :].to_broadcast([128, 8, 32])
            s0 = sinT[:, t:t + 1, 0:16].to_broadcast([128, 8, 16])
            s1 = sinT[:, t:t + 1, 16:32].to_broadcast([128, 8, 16])
            V(vec.tensor_tensor(tmp[:, :, 0:16], q3[:, :, 16:32], s0, MUL))
            V(vec.tensor_tensor(tmp[:, :, 16:32], q3[:, :, 0:16], s1, MUL))
            V.own()
            V(vec.tensor_tensor(q3, q3, co, MUL))
            V.own()
            r = V(vec.tensor_tensor(q3, q3, tmp, ADD))
            yield
            for half in range(2):
                ti, tb = yield from TB.get(P)
                P.wait(r)
                for j in range(4):
                    h = 4 * half + j
                    m = tr(tb[0:96, 128 * j:128 * j + 128], qtok[:, 96 * h:96 * h + 96], ident)
                p = P(m)
                dst = QT8[0:96, 4 * half:4 * half + 4, 128 * t:128 * t + 128]
                E = (C, V)[half]
                E.wait(p)
                view = tb[0:96, :].rearrange("p (k s) -> p k s", k=4)
                e = C(act.activation(dst, view, ACT.Copy)) if half == 0 else V(vec.tensor_copy(dst, view))
                TB.free(ti, e)
                qt_ready[t] = (*(qt_ready[t] or ()), e)
                yield
            QTOK.free(qi, p)

        run(pipeline([mla_q(t) for t in range(NT)], 3))
        V.wait(*[q for r in qt_ready for q in r])
        for i in range(4):
            t_kpe = V(vec.tensor_copy(KA[i][64:96, :], KPT))

        PB = Slots([scr(48, 1024), scr(52, 1024)])
        PTs = Slots([scr(56, 1024)])
        for e in (C, V):
            e.wait((P.sem, P.n), (V.sem, V.n))
        OGs = Slots([stats(128) for _ in range(2)])
        GT = Slots([XBa[0], XBa[1]])
        GE = Slots([XBa[2][:, 0:256], XBa[2][:, 256:512]])
        at8 = Slots([stats(8) for _ in range(6)])
        og_bufs = OGs

        def silu_into(dst, psum, z, w, read):
            gi, ge = yield from GE.get(C)
            C.wait(z)
            a = C(act.activation(ge[:, 0:w], psum, ACT.Exp, scale=-1.0))
            c = C(act.activation(dst, psum, ACT.Copy))
            read(c)
            yield
            V.wait(a, c)
            V(vec.tensor_scalar(ge[:, 0:w], ge[:, 0:w], 1.0, None, ADD))
            V.own()
            V(vec.reciprocal(ge[:, 0:w], ge[:, 0:w]))
            V.own()
            b = V(vec.tensor_tensor(dst, dst, ge[:, 0:w], MUL))
            GE.free(gi, b)
            return b

        def attend(q_of, k_of, v_of, t, key, need, done):
            n = 128 * (t + 1)
            si, sc = yield from SB.get(P)
            P.wait(*need)
            for b in range(0, n, 512):
                w = min(512, n - b)
                last = b + w == n
                m = mm(sc[:, b:b + w], q_of(t), k_of(b, w), True, not last)
            m = mm(sc[:, n - 128:n], identb[:, :], maskq[:, :], False, True)
            z = P(m)
            yield
            ai, s = yield from at8.get(V)
            V.wait(z)
            x1_ = V(vec.tensor_reduce(s[:, 0:1], sc[:, 0:n], AXX, MAX, negate=True))
            yield
            pi, pb = yield from PB.get(C)
            C.wait(x1_)
            e = C(act.activation(pb[:, 0:n], sc[:, 0:n], ACT.Exp, bias=s[:, 0:1], accum_out=s[:, 1:2]))
            SB.free(si, e)
            yield
            V.wait(e)
            rl = V(vec.reciprocal(s[:, 2:3], s[:, 1:2]))
            qi, pt = yield from PTs.get(V, C)
            evs = []
            for b in range(0, t + 1, 4):
                w = min(4, t + 1 - b)
                ti, tb = yield from TB.get(P)
                P.wait(e)
                for j in range(w):
                    m = tr(tb[:, 128 * j:128 * j + 128], pb[:, 128 * (b + j):128 * (b + j + 1)], ident)
                p = P(m)
                E = V if (b == 0) == (t < 4) else C
                E.wait(p)
                o, i_ = pt[:, 128 * b:128 * (b + w)], tb[:, 0:128 * w]
                ev = V(vec.tensor_copy(o, i_)) if E is V else C(act.activation(o, i_, ACT.Copy))
                TB.free(ti, ev)
                evs.append(ev)
            PB.free(pi, p)
            yield
            gi, bank = yield from GB.get(P)
            P.wait(*evs)
            for b in range(t + 1):
                m = mm(bank[:, 0:64], pt[:, 128 * b:128 * b + 128], v_of(b), b == 0, b == t)
            p = P(m)
            PTs.free(qi, p)
            yield
            f = yield from done(bank[:, 0:64], s[:, 2:3], p, rl)
            GB.free(gi, f)
            at8.free(ai, f)

        ot_ready = [None] * NT

        def finish_pair(pair, t, ogs, toks):
            oi, og = ogs
            ti, tb = yield from TB.get(P)
            P.wait(*toks)
            p = P(tr(tb[:, 0:128], og, ident))
            OGs.free(oi, p)
            yield
            C.wait(p)
            e = C(act.activation(OT[:, pair, 128 * t:128 * t + 128], tb[:, 0:128], ACT.Copy))
            TB.free(ti, e)
            ot_ready[t] = e

        def pair_attention(pair, q_of, k_of, v_of, gate, need, gate_ready):
            for t in range(NT):
                og = {}

                def head(h, t=t, og=og):
                    def done(o, rl, p, rl_t):
                        if h == 0:
                            og["slot"] = yield from OGs.get(V)
                        V.wait(p, rl_t, *gate_ready(t))
                        f = V(vec.scalar_tensor_tensor(og["slot"][1][:, 64 * h:64 * h + 64], o, rl,
                                                       gate[:, t, 64 * h:64 * h + 64], MUL, MUL))
                        og[h] = f
                        yield
                        if h == 1:
                            yield from finish_pair(pair, t, og["slot"], (og[0], og[1]))
                        return f

                    return attend(lambda t_: q_of(h, t_), lambda b, w: k_of(h, b, w),
                                  lambda b: v_of(h, b), t, h, need(h, t), done)

                for h in range(2):
                    yield head(h)

        kfree = {0: (), 1: (), 2: (), 3: ()}
        k_ready = {}
        g_ready = {}
        gates = {}

        def mla_prepare(p):
            gi, bank = None, None
            k_ready[p] = []
            for n in range(2):
                gi, bank = yield from GB.get(P)
                P.wait(t_wq, *lat_ready[7])
                z = P(mm(bank, wkv[:, 128 * p:128 * p + 128], CKVT[:, 512 * n:512 * n + 512], True, True))
                C.wait(z)
                for h in range(2):
                    b = 2 * (p % 2) + h
                    C.wait(*kfree[b])
                    e = C(act.activation(KA[b][0:64, 512 * n:512 * n + 512], bank[64 * h:64 * h + 64, :], ACT.Copy))
                GB.free(gi, e)
                k_ready[p].append(e)
                yield
            k_ready[p] = [*k_ready[p], t_kpe]
            yield from gate_steps(p, w_g1, 128 * p)

        def gate_steps(p, w, at):
            gt_i, gt = yield from GT.get(V, C)
            gt = gt.rearrange("p (t c) -> p t c", t=8)
            gates[p] = (gt_i, gt)
            g_ready[p] = [None] * NT
            for t in range(NT):
                gi, bank = yield from GB.get(P)
                P.wait(w[2], *ht_ready[t])
                for k in range(NK):
                    m = mm(bank[:, 0:128], HT[:, k, 128 * t:128 * t + 128], w[1][:, k, at:at + 128], k == 0, k == 7)
                z = P(m)
                b = yield from silu_into(gt[:, t, :], bank[:, 0:128], z, 128, lambda c, gi=gi: GB.free(gi, c))
                g_ready[p][t] = b
                yield

        def mla_attend(p):
            def q_of(h, t):
                return QT8[0:96, 2 * p + h, 128 * t:128 * t + 128]

            def k_of(h, b, w):
                return KA[2 * (p % 2) + h][0:96, b:b + w]

            def v_of(h, b):
                return VM[:, b, 64 * (2 * p + h):64 * (2 * p + h) + 64]

            yield from pipeline(pair_attention(
                p, q_of, k_of, v_of, gates[p][1],
                lambda h, t: [*k_ready[p], *[q for r in qt_ready[:t + 1] for q in r], *vm_ready[:t + 1]],
                lambda t: (g_ready[p][t],)), 5)
            for h in range(2):
                kfree[2 * (p % 2) + h] = ((P.sem, P.n),)
            GT.free(gates[p][0], (V.sem, V.n))

        run(mla_prepare(0))
        w_sq = wload([(wi[:, 416:928], 0)], 512)
        for p in range(4):
            if p < 3:
                run(together((mla_attend(p), 1), (mla_prepare(p + 1), 1)))
            else:
                run(mla_attend(3))
        W.free(w_g1[0], (P.sem, P.n))
        W.free(iq, (P.sem, P.n))
        W.free(vi, (P.sem, P.n))

        w_skv = wload([(wi[:, 928:1184], 0)], 256)
        w_g2 = wload([(wi[:, 1696:2208], 0)], 512)
        P.wait((C.sem, C.n), (V.sem, V.n))
        for e in (C, V):
            e.wait((P.sem, P.n))
        KS = [scr(0, 1024), scr(4, 1024)]
        VS = scr(8, 1024).rearrange("p (t c) -> p t c", t=8)
        QS = [scr(12, 1024), scr(16, 1024)]
        SW = Slots([scr(20 + 2 * i, 512) for i in range(4)])
        PW = Slots([scr(28 + 2 * i, 512) for i in range(4)])
        ks_ready = []
        for n in range(2):
            gi, bank = GB.take(P)
            P.wait(w_skv[2])
            for k in range(NK):
                m = mm(bank, w_skv[1][:, k, 0:128], HT[:, k, 512 * n:512 * n + 512], k == 0, k == 7)
            z = P(m)
            C.wait(z)
            for g in range(2):
                for h in range(2):
                    e = C(act.activation(KS[g][64 * h:64 * h + 64, 512 * n:512 * n + 512],
                                         bank[64 * g:64 * g + 64, :], ACT.Copy))
            GB.free(gi, e)
            ks_ready.append(e)
        for t in range(NT):
            gi, bank = GB.take(P)
            for k in range(NK):
                m = mm(bank[:, 0:128], HT[:, k, 128 * t:128 * t + 128], w_skv[1][:, k, 128:256], k == 0, k == 7)
            z = P(m)
            C.wait(z)
            e = C(act.activation(VS[:, t, :], bank[:, 0:128], ACT.Copy))
            GB.free(gi, e)
        ks_ready.append(e)
        W.free(w_skv[0], (P.sem, P.n))
        qs_ready = {}
        qs_free = {0: (), 1: ()}
        DM = CST[:, C_DM:C_DM + 256]

        def swa_prepare(p):
            qs_ready[p] = []
            for n in range(2):
                gi, bank = yield from GB.get(P)
                P.wait(w_sq[2])
                for k in range(NK):
                    m = mm(bank, w_sq[1][:, k, 128 * p:128 * p + 128], HT[:, k, 512 * n:512 * n + 512],
                           k == 0, k == 7)
                z = P(m)
                C.wait(z, *qs_free[p % 2])
                e = C(act.activation(QS[p % 2][:, 512 * n:512 * n + 512], bank, ACT.Copy, scale=0.125))
                GB.free(gi, e)
                qs_ready[p].append(e)
                yield
            yield from gate_steps(4 + p, w_g2, 128 * p)

        def swa_block(p, t):
            lo = 128 if t == 0 else 0
            k0 = 128 * t - 128 + lo
            w = 256 - lo
            si, sc = yield from SB.get(P)
            P.wait(*qs_ready[p], *ks_ready)
            for h in range(2):
                m = mm(sc[:, 512 * h + lo:512 * h + 256], QS[p % 2][64 * h:64 * h + 64, 128 * t:128 * t + 128],
                       KS[p // 2][64 * h:64 * h + 64, k0:k0 + w], True, True)
            z = P(m)
            yield
            wi_, sw = yield from SW.get(V, C)
            ai, s = yield from at8.get(V)
            V.wait(z)
            sw3 = sw.rearrange("p (h c) -> p h c", h=2)
            for h in range(2):
                slope = 2.0 ** -(2 * p + h + 1)
                b = V(vec.scalar_tensor_tensor(sw3[:, h, lo:256], DM[:, lo:256], -slope,
                                               sc[:, 512 * h + lo:512 * h + 256], MUL, ADD))
            SB.free(si, b)
            V.wait(b)
            V(vec.tensor_reduce(s[:, 0:2], sw3[:, :, lo:256], AXX, MAX))
            V.own()
            V.wait(t_snk)
            V(vec.tensor_tensor(s[:, 0:2], s[:, 0:2], snk[:, 2 * p:2 * p + 2], MAX))
            V.own()
            V(vec.tensor_tensor(s[:, 2:4], snk[:, 2 * p:2 * p + 2], s[:, 0:2], SUB))
            a = V(vec.tensor_scalar(s[:, 0:2], s[:, 0:2], -1.0, None, MUL))
            yield
            pi, pw = yield from PW.get(C, V)
            C.wait(a)
            for h in range(2):
                C(act.activation(sw3[:, h, lo:256], sw3[:, h, lo:256], ACT.Exp, bias=s[:, h:h + 1],
                                 accum_out=s[:, 4 + h:5 + h]))
            e = C(act.activation(s[:, 2:4], s[:, 2:4], ACT.Exp))
            yield
            V.wait(e)
            V(vec.tensor_tensor(s[:, 4:6], s[:, 4:6], s[:, 2:4], ADD))
            V.own()
            rl = V(vec.reciprocal(s[:, 6:8], s[:, 4:6]))
            ti, tb = yield from TB.get(P)
            P.wait(e)
            blocks = [1] if t == 0 else [0, 1]
            for h in range(2):
                for c in blocks:
                    m = tr(tb[:, 256 * h + 128 * c:256 * h + 128 * c + 128],
                                     sw3[:, h, 128 * c:128 * c + 128], ident)
            p_ = P(m)
            SW.free(wi_, p_)
            C.wait(p_)
            ev = C(act.activation(pw.rearrange("p (h c) -> p h c", h=2)[:, :, lo:256],
                                  tb.rearrange("p (h c) -> p h c", h=2)[:, :, lo:256], ACT.Copy))
            TB.free(ti, ev)
            yield
            gi, bank = yield from GB.get(P)
            P.wait(ev)
            kv = p // 2
            for h in range(2):
                for c in blocks:
                    m = mm(bank[:, 64 * h:64 * h + 64], pw[:, 256 * h + 128 * c:256 * h + 128 * c + 128],
                           VS[:, t - 1 + c, 64 * kv:64 * kv + 64], c == blocks[0], c == 1)
            o = P(m)
            PW.free(pi, o)
            yield
            og = yield from OGs.get(V)
            V.wait(o, rl, g_ready[4 + p][t])
            for h in range(2):
                f = V(vec.scalar_tensor_tensor(og[1][:, 64 * h:64 * h + 64], bank[:, 64 * h:64 * h + 64],
                                               s[:, 6 + h:7 + h], gates[4 + p][1][:, t, 64 * h:64 * h + 64],
                                               MUL, MUL))
            GB.free(gi, f)
            at8.free(ai, f)
            yield
            yield from finish_pair(4 + p, t, og, (f,))

        def swa_attend(p):
            yield from pipeline((swa_block(p, t) for t in range(NT)), 5)
            qs_free[p % 2] = ((P.sem, P.n),)
            GT.free(gates[4 + p][0], (V.sem, V.n))

        run(swa_prepare(0))
        w_o = [wload([(e_w_out[0][:, 0:512], 0)], 512)]
        for p in range(4):
            if p < 3:
                run(together((swa_attend(p), 1), (swa_prepare(p + 1), 1)))
            else:
                run(swa_attend(3))
        W.free(w_sq[0], (P.sem, P.n))
        W.free(w_g2[0], (P.sem, P.n))
        w_o.append(wload([(e_w_out[0][:, 512:1024], 0)], 512))

        def all_engines_meet():
            toks = [(e.sem, e.n) for e in (P, C, V)] + [t for t in stores() if t[1]]
            for e in (P, C, V, Y, G):
                e.wait(*toks)

        def reuse_x():
            XB.freed = [()] * 3
            XB.at = 0
            XN.freed = [()] * 2
            XN.at = 0

        def project_out(t, w_o, xl):
            si, sb2 = SB.take(P)
            for n in range(2):
                P.wait(w_o[n][2])
                for k in range(NK):
                    m = mm(sb2[:, 512 * n:512 * n + 512], OT[:, k, 128 * t:128 * t + 128], w_o[n][1][:, k, :],
                           k == 0, k == 7)
            return si, sb2, P(m)

        def after_first(t, w_o, src, dst, gain, t_gain, store_norm):
            i, buf, tx = xload[t]
            si, sb2, z = project_out(t, w_o, None)
            yield
            V.wait(z, tx)
            r = V(vec.tensor_tensor(buf, buf, sb2, ADD))
            SB.free(si, r)
            keep = []
            if dst is not None:
                Y.wait(r)
                keep.append(c_sx[i](sync.dma_start(dst[128 * t:128 * t + 128, :], buf)))

            def release(n):
                XB.free(i, n, *keep)
                if t + 3 < NT:
                    xload[t + 3] = load_x(src, t + 3)

            yield
            yield from rms_entry(t, buf, [r], gain, t_gain, release, store_norm)

        all_engines_meet()
        reuse_x()
        GN = scr(48, 1024)
        t_g = once(bcast_row(GN, o_g_in[0]))
        for t in range(3):
            xload[t] = load_x(xin, t)
        run(pipeline([after_first(t, w_o, xin, x1, GN, t_g, None) for t in range(NT)], 3))
        for w in w_o:
            W.free(w[0], (P.sem, P.n))
        x1_done = stores()

        all_engines_meet()
        wo_ = o_w_in[0]
        t_wf = once((WF[:, :, 0:16], wo_[:, 3072:3088].rearrange("(k p) c -> p k c", p=128)))
        bfc = stats(1)
        t_bf = once((bfc[0:16, :], o_b_f[0].rearrange("(p a) -> p a", a=1)))

        def fox_weights(p):
            return wload([(wo_[:, 128 * p:128 * p + 128], 0), (wo_[:, 1024 + 128 * p:1152 + 128 * p], 128),
                          (wo_[:, 2048 + 128 * p:2176 + 128 * p], 256),
                          (wo_[:, 3088 + 128 * p:3216 + 128 * p], 384)], 512)

        fw = {p: fox_weights(p) for p in range(3)}
        QA = [scr(4 * i, 1024) for i in range(4)]
        KA = [scr(16 + 4 * i, 1024) for i in range(4)]
        VG = [scr(32 + 8 * i, 2048).rearrange("p (t c) -> p t c", t=8) for i in range(2)]
        PB = Slots([scr(48, 1024), scr(52, 1024)])
        PTs = Slots([scr(56, 1024)])
        GE = Slots([XBa[2][:, 0:256], XBa[2][:, 256:512]])
        LC = XBa[0]
        NLC = XBa[1]

        def log_sigmoid(x_, e_, n):
            V(vec.scalar_tensor_tensor(e_, x_, -1.0, x_, MUL, MAX))
            C.wait((V.sem, V.n))
            C(act.activation(e_, e_, ACT.Exp, scale=-1.0))
            C.own()
            a = C(act.activation(e_, e_, ACT.Ln, bias=1.0))
            V.wait(a)
            return V(vec.scalar_tensor_tensor(x_, x_, 0.0, e_, MIN, SUB))

        for n in range(2):
            gi, bank = GB.take(P)
            P.wait(t_wf, *[q for r in ht_ready for q in r])
            for k in range(NK):
                m = mm(bank[0:16, :], WF[:, k, 0:16], HT[:, k, 512 * n:512 * n + 512], k == 0, k == 7)
            z = P(m)
            V.wait(z, t_bf)
            e = V(vec.tensor_scalar(LC[0:16, 512 * n:512 * n + 512], bank[0:16, :], bfc[0:16, :], None, ADD))
            GB.free(gi, e)
        V.own()
        log_sigmoid(LC[0:16, :], NLC[0:16, :], 1024)
        zz = XBa[2][0:16, :]
        V(vec.memset(zz, 1.0))
        V.own()
        t_c = V(vec.tensor_tensor_scan(LC[0:16, :], zz, LC[0:16, :], 0.0, MUL, ADD))
        V.own()
        t_nc = V(vec.tensor_scalar(NLC[0:16, :], LC[0:16, :], -1.0, None, MUL))
        for i in range(4):
            V(vec.memset(QA[i][64:66, :], 1.0))
            t_ones = V(vec.memset(KA[i][64:66, :], 1.0))
        C.wait(t_nc)
        Y.wait(t_nc, t_ones)
        c_aug = [Counter(sem()) for _ in range(4)]
        qkfree = {0: (), 1: ()}
        vg_free = {0: (), 1: ()}
        fq_ready, fv_ready, faug = {}, {}, {}

        def fox_prepare(p):
            w = fw[p]
            par = p % 2
            Y.wait(*qkfree[par])
            faug[p] = []
            for h in range(2):
                b = 2 * par + h
                c_aug[b](sync.dma_start(QA[b][64:65, :], LC[2 * p + h:2 * p + h + 1, :]))
                faug[p].append(c_aug[b](sync.dma_start(KA[b][65:66, :], NLC[2 * p + h:2 * p + h + 1, :])))
            fq_ready[p] = []
            for which, bufs, scale in ((0, QA, 0.125), (1, KA, 1.0)):
                for n in range(2):
                    gi, bank = yield from GB.get(P)
                    P.wait(w[2])
                    for k in range(NK):
                        m = mm(bank, w[1][:, k, 128 * which:128 * which + 128], HT[:, k, 512 * n:512 * n + 512],
                               k == 0, k == 7)
                        if k == 3:
                            yield
                    z = P(m)
                    C.wait(z, *qkfree[par])
                    for h in range(2):
                        e = C(act.activation(bufs[2 * par + h][0:64, 512 * n:512 * n + 512],
                                             bank[64 * h:64 * h + 64, :], ACT.Copy, scale=scale))
                    GB.free(gi, e)
                    fq_ready[p].append(e)
                    yield
            fv_ready[p] = [None] * NT
            for t in range(NT):
                gi, bank = yield from GB.get(P)
                for k in range(NK):
                    m = mm(bank[:, 0:256], HT[:, k, 128 * t:128 * t + 128], w[1][:, k, 256:512], k == 0, k == 7)
                    if k == 3:
                        yield
                z = P(m)
                C.wait(z, *vg_free[par])
                V.wait(*vg_free[par])
                C(act.activation(VG[par][:, t, 0:128], bank[:, 0:128], ACT.Copy))
                a = (C.sem, C.n)
                b = yield from silu_into(VG[par][:, t, 128:256], bank[:, 128:256], z, 128,
                                         lambda c, gi=gi: GB.free(gi, c))
                fv_ready[p][t] = (a, b)
                yield
            W.free(w[0], (P.sem, P.n))
            if p + 3 < 8:
                fw[p + 3] = fox_weights(p + 3)

        def fox_attend(p):
            par = p % 2

            def q_of(h, t):
                return QA[2 * par + h][0:66, 128 * t:128 * t + 128]

            def k_of(h, b, w):
                return KA[2 * par + h][0:66, b:b + w]

            def v_of(h, b):
                return VG[par][:, b, 64 * h:64 * h + 64]

            yield from pipeline(pair_attention(
                p, q_of, k_of, v_of, VG[par][:, :, 128:256],
                lambda h, t: [*faug[p], *fq_ready[p], *[r[0] for r in fv_ready[p][:t + 1]]],
                lambda t: (fv_ready[p][t][1],)), 5)
            qkfree[par] = ((P.sem, P.n),)
            vg_free[par] = ((P.sem, P.n), (V.sem, V.n))

        run(fox_prepare(0))
        for p in range(8):
            if p < 7:
                run(together((fox_attend(p), 1), (fox_prepare(p + 1), 1)))
            else:
                w_o = [wload([(o_w_out[0][:, 512 * n:512 * n + 512], 0)], 512) for n in range(2)]
                run(fox_attend(p))

        all_engines_meet()
        reuse_x()
        GN = scr(48, 1024)
        t_g = once(bcast_row(GN, g_final))
        Y.wait(*x1_done)
        for t in range(3):
            xload[t] = load_x(x1, t)
        run(pipeline([after_first(t, w_o, x1, None, GN, t_g, x2) for t in range(NT)], 3))
        for w in w_o:
            W.free(w[0], (P.sem, P.n))
        x2_done = stores()

        all_engines_meet()
        wm = w_in_2[0]
        V(vec.memset(WF[:, :, :], 0.0))
        Y.wait((V.sem, V.n))
        t_wf = once((WF[:, :, 0:4], wm[:, 2048:2052].rearrange("(k p) c -> p k c", p=128)),
                    (WF[:, :, 32:36], wm[:, 2052:2056].rearrange("(k p) c -> p k c", p=128)))
        bic = stats(2)
        CW = stats(32).rearrange("p (k j) -> p k j", k=8)
        PSC = stats(4)
        t_small = once((bic[0:4, 0:1], b_i_2[0].rearrange("(p a) -> p a", a=1)),
                       (bic[0:4, 1:2], b_f_2[0].rearrange("(p a) -> p a", a=1)),
                       (PSC, pool_scale_2[0].rearrange("(g p) -> p g", p=128)),
                       *[(CW[:, :, j], conv_qk_2[0][j].rearrange("(k p) -> p k", p=128)) for j in range(4)])

        def mix_weights(h):
            return wload([(wm[:, 512 * j + 128 * h:512 * j + 128 * h + 128], 128 * j) for j in range(4)], 512)

        mw = {h: mix_weights(h) for h in range(4)}
        XW = A[:, 32 * KW * 2 + 64 * KW:32 * KW * 2 + 76 * KW]
        CV = [(OT[:, 4, :], OT[:, 5, :]), (scr(4.5, 1024), scr(8.5, 1024))]
        VO = [v.rearrange("p (t c) -> p t c", t=8) for v in (XW[:, 0:2080], scr(16.5, 2080))]
        KTm = [v.rearrange("p (t c) -> p t c", t=8) for v in (OT[:, 6, :], scr(25, 1024))]
        WBC = [OT[:, 7, :], scr(37, 1024)]
        ZB = scr(0, 1028)
        EX = scr(12.5, 1024)
        GR = scr(29, 1024)
        GC = scr(33, 1024).rearrange("p (t c) -> p t c", t=8)
        T0 = scr(41, 1024)
        T1 = scr(45, 1024)
        HG = scr(49, 512)
        EM = Slots([scr(51 + 0.5 * i, 128) for i in range(3)] + [scr(53.5 + 0.5 * i, 128) for i in range(1)])
        CS = scr(52.5, 132)
        NUM = Slots([XW[:, 2080 + 160 * i:2240 + 160 * i] for i in range(5)])
        HN = Slots([scr(54 + 0.5 * i, 128) for i in range(4)])
        SOb = scr(56.5, 32)
        SO4 = scr(57, 32)
        MP = scr(57.25, 8)
        SO = scr(57.5, 8)
        SEL = scr(58, 512)
        t_hg = once(bcast_row(HG, head_norm_g_2[0]))

        IG, LF = T0[0:4, :], T1[0:4, :]
        EXg = KTm[1].rearrange("p t c -> p (t c)")
        m_row = CV[1][0][0:4, :]
        b_row = CV[1][1][0:4, :]
        dif = WBC[1][0:4, :]
        WROW = scr(16.5, 1024)[0:4, :]
        ones_r = T0[0:4, :]
        gates = {}

        def mix_gates():
            for n in range(2):
                gi, bank = yield from GB.get(P)
                P.wait(t_wf)
                for k in range(NK):
                    m = mm(bank[0:36, :], WF[:, k, :], HT[:, k, 512 * n:512 * n + 512], k == 0, k == 7)
                z = P(m)
                V.wait(z, t_small)
                V(vec.tensor_scalar(T0[0:4, 512 * n:512 * n + 512], bank[0:4, :], bic[0:4, 0:1], None, ADD))
                e = V(vec.tensor_scalar(T1[0:4, 512 * n:512 * n + 512], bank[32:36, :], bic[0:4, 1:2], None, ADD))
                GB.free(gi, e)
            V.own()
            eg = EXg[0:4, :]
            V(vec.scalar_tensor_tensor(eg, LF, -1.0, LF, MUL, MAX))
            C.wait((V.sem, V.n))
            C(act.activation(eg, eg, ACT.Exp, scale=-1.0))
            C.own()
            a = C(act.activation(eg, eg, ACT.Ln, bias=1.0))
            V(vec.memset(GR, 0.0))
            V(vec.memset(WROW, 1.0))
            V(vec.memset(SEL[0:4, :], 0.0))
            V(vec.memset(MP[0:4, 0:1], 0.0))
            V.own()
            V(vec.memset(WROW.rearrange("p (t c) -> p t c", t=8)[:, :, 0:1], 0.0))
            V(vec.tensor_copy(SEL[0:4, :].rearrange("p (h c) -> p h c", h=4),
                              CST[0:4, C_BD:C_BD + 32].rearrange("p (h c) -> p h c", h=4)[:, :, 0:1]
                              .to_broadcast([4, 4, 128])))
            yield
            V.wait(a)
            V(vec.scalar_tensor_tensor(LF, LF, 0.0, eg, MIN, SUB))
            V.own()
            V(vec.tensor_tensor_scan(m_row, LF, IG, 0.0, ADD, MAX))
            V(vec.tensor_tensor_scan(b_row, WROW, LF, 0.0, MUL, ADD))
            m3 = m_row.rearrange("p (t c) -> p t c", t=8)
            b3 = b_row.rearrange("p (t c) -> p t c", t=8)
            V.own()
            V(vec.tensor_copy(MP[0:4, 1:8], m3[:, 0:7, 127]))

            def g3(a):
                return GR[a:a + 4, :].rearrange("p (t c) -> p t c", t=8)

            def rep(v):
                return v.to_broadcast([4, 8, 128])

            mp3 = MP[0:4, :].rearrange("p (t c) -> p t c", c=1)
            V(vec.tensor_tensor(g3(0), IG.rearrange("p (t c) -> p t c", t=8), b3, SUB))
            V(vec.tensor_tensor(dif, b_row, m_row, SUB))
            V(vec.tensor_scalar(GR[64:68, :], m_row, -1.0, None, MUL))
            V(vec.tensor_tensor(SO[0:4, :], b3[:, :, 127], m3[:, :, 127], SUB))
            V.own()
            V(vec.memset(ones_r[:, 0:128], 1.0))
            V(vec.tensor_tensor(g3(32), dif.rearrange("p (t c) -> p t c", t=8), rep(mp3), ADD))
            so3 = SO[0:4, :].rearrange("p (t c) -> p t c", c=1)
            V(vec.tensor_tensor(g3(96), g3(0), rep(so3), ADD))
            V.own()
            V(vec.tensor_tensor(SO[0:4, :], SO[0:4, :], MP[0:4, :], ADD))
            V.own()
            C.wait((V.sem, V.n))
            e = C(act.activation(SO[0:4, :], SO[0:4, :], ACT.Exp))
            V(vec.tensor_copy(T1[0:4, :], dif))
            yield
            V.wait(e)
            so_b = SO[0:4, :].rearrange("p (h c) -> p h c", h=1).to_broadcast([4, 4, 8])
            t_rows = V(vec.tensor_tensor(SO4[0:4, :].rearrange("p (h c) -> p h c", h=4), so_b,
                                         CST[0:4, C_BD:C_BD + 32].rearrange("p (h c) -> p h c", h=4), MUL))
            for half in range(2):
                ti, tb = yield from TB.get(P)
                P.wait(t_rows)
                for j in range(4):
                    t = 4 * half + j
                    m = tr(tb[:, 128 * j:128 * j + 128], GR[:, 128 * t:128 * t + 128], ident)
                z = P(m)
                tv = tb.rearrange("p (t c) -> p t c", t=4)
                V.wait(z)
                c = V(vec.tensor_copy(GC[:, 4 * half:4 * half + 4, 0:4], tv[:, :, 0:4]))
                C.wait(c)
                e = C(act.activation(GC[:, 4 * half:4 * half + 4, 32:128], tv[:, :, 32:128], ACT.Exp))
                TB.free(ti, e)
            gi, bank = yield from GB.get(P)
            z = P(mm(bank[:, 0:32], ones_r[:, 0:128], SO4[0:4, :], True, True))
            V.wait(z, e)
            gates["done"] = V(vec.tensor_copy(SOb, bank[:, 0:32]))
            GB.free(gi, gates["done"])

        SCALE_M = 128.0 ** -0.5
        V(vec.memset(ZB[:, 0:3], 0.0))
        V(vec.memset(VO[0][:, :, 128:129], 1.0))
        t_z = ((V.sem, V.n),)
        qk_free = [t_z, t_z]
        head_done = {}
        head_ready = {}
        after_head = {}

        def mix_prepare(h):
            w = mw[h]
            old = head_done.get(h - 2, ())
            cvs, vo, kt, wb = CV[h % 2], VO[h % 2], KTm[h % 2], WBC[h % 2]
            for which in range(2):
                ch = 4 * which + h
                for n in range(2):
                    gi, bank = yield from GB.get(P)
                    P.wait(w[2])
                    for k in range(NK):
                        m = mm(bank, w[1][:, k, 128 * which:128 * which + 128], HT[:, k, 512 * n:512 * n + 512],
                               k == 0, k == 7)
                    z = P(m)
                    C.wait(z, *qk_free[0])
                    e = C(act.activation(ZB[:, 3 + 512 * n:515 + 512 * n], bank, ACT.Copy))
                    GB.free(gi, e)
                    yield
                while which == 1 and h == 1 and "done" not in gates:
                    yield
                V.wait(e, *old)
                cv = cvs[which]
                V(vec.tensor_scalar(cv, ZB[:, 0:1024], CW[:, ch, 0:1], None, MUL))
                for j in range(1, 4):
                    V.own()
                    c = V(vec.scalar_tensor_tensor(cv, ZB[:, j:j + 1024], CW[:, ch, j:j + 1], cv, MUL, ADD))
                qk_free[0] = (c,)
                C.wait(c, *qk_free[1])
                e = C(act.activation(EX, cv, ACT.Exp, scale=-1.0))
                yield
                V.wait(e)
                V(vec.tensor_scalar(EX, EX, 1.0, None, ADD))
                V.own()
                V(vec.reciprocal(EX, EX))
                V.own()
                t_qk = V(vec.tensor_tensor(cv, cv, EX, MUL))
                qk_free[1] = (t_qk,)
                yield
            C.wait(*old)
            for t in range(NT):
                gi, bank = yield from GB.get(P)
                for k in range(NK):
                    m = mm(bank[:, 0:256], HT[:, k, 128 * t:128 * t + 128], w[1][:, k, 256:512], k == 0, k == 7)
                z = P(m)
                C.wait(z)
                C(act.activation(vo[:, t, 0:128], bank[:, 0:128], ACT.Copy))
                e = C(act.activation(vo[:, t, 130:258], bank[:, 128:256], ACT.Exp, scale=-1.0))
                GB.free(gi, e)
                yield
                V.wait(e)
                V(vec.tensor_scalar(vo[:, t, 130:258], vo[:, t, 130:258], 1.0, None, ADD))
                V.own()
                t_vo = V(vec.reciprocal(vo[:, t, 130:258], vo[:, t, 130:258]))
            W.free(w[0], z)
            after_head[h]()
            while "done" not in gates:
                yield
            P.wait(gates["done"])
            for n in range(2):
                gi, bank = yield from GB.get(P)
                z = P(mm(bank, SEL[0:4, 128 * h:128 * h + 128], T1[0:4, 512 * n:512 * n + 512], True, True))
                V.wait(z)
                e = V(vec.tensor_copy(wb[:, 512 * n:512 * n + 512], bank))
                GB.free(gi, e)
                yield
            for half in range(2):
                ti, tb = yield from TB.get(P)
                P.wait(t_qk)
                for j in range(4):
                    t = 4 * half + j
                    m = tr(tb[:, 128 * j:128 * j + 128], cvs[1][:, 128 * t:128 * t + 128], ident)
                z = P(m)
                V.wait(z)
                for j in range(4):
                    t = 4 * half + j
                    e = V(vec.tensor_scalar(kt[:, t, :], tb[:, 128 * j:128 * j + 128],
                                            GC[:, t, 96 + h:97 + h], None, MUL))
                TB.free(ti, e)
                yield
            head_ready[h] = (t_qk, t_vo, e)

        def mix_chunks(h):
            cvs, vo, kt, wb = CV[h % 2], VO[h % 2], KTm[h % 2], WBC[h % 2]
            P.wait(*head_ready[h])
            V.wait(*head_ready[h])
            state = [0, V(vec.memset(CS, 0.0))]
            V.own()

            def chunk(t):
                ei, em = yield from EM.get(V, C)
                a = V(vec.tensor_tensor(em, wb[:, 128 * t:128 * t + 128], CST[:, C_MT:C_MT + 128], ADD))
                C.wait(a)
                e = C(act.activation(em, em, ACT.Exp, bias=GC[:, t, h:h + 1]))
                si, sc = yield from SB.get(P)
                z = P(mm(sc[:, 0:128], cvs[1][:, 128 * t:128 * t + 128], cvs[0][:, 128 * t:128 * t + 128], True, True))
                yield
                V.wait(z, e)
                a = V(vec.scalar_tensor_tensor(em, sc[:, 0:128], SCALE_M, em, MUL, MUL))
                SB.free(si, a)
                yield
                while state[0] != t:
                    yield
                gi, bank = yield from GB.get(P)
                P.wait(a)
                z1 = P(mm(bank[:, 0:129], em, vo[:, t, 0:129], True, True))
                EM.free(ei, z1)
                si, sc = yield from SB.get(P)
                mm(sc[:, 512:512 + 129], kt[:, t, :], vo[:, t, 0:129], True, True)
                P.wait(state[1])
                z2 = P(mm(sc[:, 0:129], cvs[0][:, 128 * t:128 * t + 128], CS[:, 0:129], True, True))
                yield
                ni, nb = yield from NUM.get(V)
                num, s = nb[:, 0:132], nb[:, 136:152]
                V.wait(z1, z2)
                a = V(vec.scalar_tensor_tensor(CS[:, 0:129], CS[:, 0:129], SOb[:, 8 * h + t:8 * h + t + 1],
                                               sc[:, 512:512 + 129], MUL, ADD))
                state[:] = [t + 1, a]
                a = V(vec.tensor_scalar(num[:, 0:129], sc[:, 0:129], GC[:, t, 32 + h:33 + h], SCALE_M, MUL, MUL))
                SB.free(si, a)
                V.own()
                a = V(vec.tensor_tensor(num[:, 0:129], num[:, 0:129], bank[:, 0:129], ADD))
                GB.free(gi, a)
                V.own()
                V(vec.scalar_tensor_tensor(s[:, 0:1], num[:, 128:129], -1.0, num[:, 128:129], MUL, MAX))
                V.own()
                V(vec.tensor_tensor(s[:, 0:1], s[:, 0:1], GC[:, t, 64 + h:65 + h], MAX))
                V.own()
                V(vec.reciprocal(s[:, 0:1], s[:, 0:1]))
                V.own()
                V(vec.tensor_scalar(num[:, 0:128], num[:, 0:128], s[:, 0:1], None, MUL))
                V.own()
                V(vec.bn_stats(s[:, 1:7], num[:, 0:128]))
                V.own()
                V(vec.bn_aggr(s[:, 8:10], s[:, 1:7]))
                V.own()
                b = V(vec.tensor_scalar(s[:, 10:11], s[:, 9:10], LN_EPS, None, ADD))
                yield
                rsqrt(s[:, 10:11], s[:, 11:12], b)
                V(vec.tensor_scalar(num[:, 0:128], num[:, 0:128], s[:, 8:9], s[:, 11:12], SUB, MUL))
                V.own()
                V.wait(t_hg)
                V(vec.tensor_tensor(num[:, 0:128], num[:, 0:128], HG[:, 128 * h:128 * h + 128], MUL))
                V.own()
                hi, hn = yield from HN.get(V)
                a = V(vec.tensor_tensor(hn, num[:, 0:128], vo[:, t, 130:258], MUL))
                NUM.free(ni, a)
                ti, tb = yield from TB.get(P)
                P.wait(a)
                z = P(tr(tb[:, 0:128], hn, ident))
                HN.free(hi, z)
                C.wait(z)
                e = C(act.activation(OT[:, h, 128 * t:128 * t + 128], tb[:, 0:128], ACT.Copy))
                TB.free(ti, e)
                yield

            yield from pipeline((chunk(t) for t in range(NT)), MIXW)
            head_done[h] = ((P.sem, P.n), (C.sem, C.n), (V.sem, V.n))

        MIXW = 4
        pw = {}

        def load_pools():
            pw["in"] = wload([(wm[:, 2056:2568], 0)], 512)

        def load_pool_mix():
            pw["mix"] = wload([(pool_w_2[0].rearrange("g c d -> (g c) d"), 0)], 128)

        def load_out():
            pw.setdefault("out", []).append(
                wload([(w_mix_out_2[0][:, 512 * n:512 * n + 512], 0) for n in (len(pw.get("out", ())),)], 512))

        after_head = {0: load_pools, 1: load_pool_mix, 2: load_out, 3: load_out}

        def pools():
            wi_p, wp, t_wp = pw["in"]
            ip, pw_, t_pw = pw["mix"]
            U = Slots([EX, GR])
            bufs = [T0, scr(45, 1024)]
            pb_ = ZB[:, 0:1024]
            old = head_done[2]
            t_pb = [(P.sem, P.n)]
            V.wait(*t_pb)
            C.wait(*qk_free[0], *qk_free[1])
            for g in range(4):
                ui, u = yield from U.get(C)
                for n in range(2):
                    gi, bank = yield from GB.get(P)
                    P.wait(t_wp)
                    for k in range(NK):
                        m = mm(bank, wp[:, k, 128 * g:128 * g + 128], HT[:, k, 512 * n:512 * n + 512], k == 0, k == 7)
                    z = P(m)
                    C.wait(z)
                    e = C(act.activation(u[:, 512 * n:512 * n + 512], bank, ACT.Copy))
                    GB.free(gi, e)
                    yield
                V.wait(e)
                cur = u
                win = 2 ** (g + 1)
                sh = 1
                bi = 0
                while sh < win:
                    o = bufs[bi]
                    V(vec.tensor_copy(o[:, 0:sh], cur[:, 0:sh]))
                    V(vec.tensor_tensor(o[:, sh:1024], cur[:, sh:1024], cur[:, 0:1024 - sh], ADD))
                    V.own()
                    cur = o
                    bi ^= 1
                    sh *= 2
                    yield
                V(vec.tensor_tensor(cur[:, 0:16], cur[:, 0:16], CST[:, C_IC + 16 * g:C_IC + 16 * g + 16], MUL))
                V.own()
                V.wait(*t_pb, *old)
                V(vec.tensor_tensor(pb_[:, 0:16], cur[:, 0:16], u[:, 0:16], SUB))
                e = V(vec.scalar_tensor_tensor(pb_[:, 16:1024], cur[:, 16:1024], 1.0 / win, u[:, 16:1024], MUL, SUB))
                V.own()
                U.free(ui, e)
                yield
                for n in range(2):
                    gi, bank = yield from GB.get(P)
                    P.wait(t_pw, e)
                    z = P(mm(bank, pw_[:, g, :], pb_[:, 512 * n:512 * n + 512], True, True))
                    V.wait(z)
                    f = V(vec.tensor_scalar(OT[:, 4 + g, 512 * n:512 * n + 512], bank, PSC[:, g:g + 1], None, MUL))
                    GB.free(gi, f)
                    yield
                t_pb = [z]
            W.free(wi_p, z)
            W.free(ip, z)

        def first_head():
            yield from together((mix_gates(), 1), (mix_prepare(0), 1))
            V(vec.memset(VO[1][:, :, 128:129], 1.0))

        run(first_head())
        for h in range(4):
            run(together((mix_chunks(h), 2), (mix_prepare(h + 1) if h < 3 else pools(), 1)))
        w_o = pw["out"]

        lnst = [stats(18) for _ in range(3)]

        def layer_norm(t, yb, t_y, gb, bb, t_gb, xn):
            s = lnst[t % 3]
            V.wait(t_y)
            for h in range(2):
                V(vec.bn_stats(s[:, 6 * h:6 * h + 6], yb[:, 512 * h:512 * h + 512]))
            V.own()
            V(vec.bn_aggr(s[:, 12:14], s[:, 0:12]))
            V.own()
            b = V(vec.tensor_scalar(s[:, 14:15], s[:, 13:14], LN_EPS, None, ADD))
            yield
            rsqrt(s[:, 14:15], s[:, 15:16], b)
            V(vec.tensor_scalar(xn, yb, s[:, 12:13], s[:, 15:16], SUB, MUL))
            V.own()
            V.wait(t_gb)
            V(vec.tensor_tensor(xn, xn, gb, MUL))
            V.own()
            return V(vec.tensor_tensor(xn, xn, bb, ADD))

        def after_ln(t, w_o, src, dst, gb, bb, t_gb):
            i, buf, tx = xload[t]
            si, sb2, z = project_out(t, w_o, None)
            yield
            V.wait(z, tx)
            r = V(vec.scalar_tensor_tensor(buf, buf, ALPHA, sb2, MUL, ADD))
            SB.free(si, r)
            ni, xn = yield from XN.get(V)
            n = yield from layer_norm(t, buf, r, gb, bb, t_gb, xn)
            XB.free(i, n)
            if t + 3 < NT:
                xload[t + 3] = load_x(src, t + 3)
            yield
            toks = yield from to_feature_major(xn, cols(HT, t), n, t % 2)
            Y.wait(n)
            st = c_sn[ni](sync.dma_start(dst[128 * t:128 * t + 128, :], xn))
            XN.free(ni, toks[0], st)
            ht_ready[t] = toks[1:]

        all_engines_meet()
        reuse_x()
        GN, BN = scr(44, 1024), scr(48, 1024)
        t_g = once(bcast_row(GN, ln_mix_g_2[0]), bcast_row(BN, ln_mix_b_2[0]))
        Y.wait(*x2_done)
        for t in range(3):
            xload[t] = load_x(x2, t)
        run(pipeline([after_ln(t, w_o, x2, x3, GN, BN, t_g) for t in range(NT)], 3))
        for w in w_o:
            W.free(w[0], (P.sem, P.n))
        x1_done = stores()

        all_engines_meet()
        MEM = scr(0, 2048).rearrange("p (t c) -> p t c", t=2)
        MT = scr(8, 2048).rearrange("p (k s) -> p k s", k=8)
        KX = scr(16, 2048).rearrange("p (k s) -> p k s", k=8)
        VX = scr(24, 2048).rearrange("p (t c) -> p t c", t=2)
        t_mem = once((MEM, mem_2[0].rearrange("(t p) c -> p t c", p=128)))
        wx = [wload([(w_xkv_2[0][:, 512 * j:512 * j + 512], 0)], 512) for j in range(3)]
        for t in range(2):
            run_ = to_feature_major(MEM[:, t, :], MT[:, :, 128 * t:128 * t + 128], t_mem, t)
            run(run_)
        P.wait((C.sem, C.n), (V.sem, V.n))
        for j in range(2):
            for c in range(4):
                gi, bank = GB.take(P)
                P.wait(wx[j][2])
                for k in range(NK):
                    m = mm(bank[:, 0:256], wx[j][1][:, k, 128 * c:128 * c + 128], MT[:, k, :], k == 0, k == 7)
                z = P(m)
                C.wait(z)
                e = C(act.activation(KX[:, 4 * j + c, :], bank[:, 0:256], ACT.Copy))
                GB.free(gi, e)
            W.free(wx[j][0], (P.sem, P.n))
            if j == 0:
                wx.append(wload([(w_xkv_2[0][:, 1536:2048], 0)], 512))
        for j in range(2):
            for t in range(2):
                gi, bank = GB.take(P)
                P.wait(wx[2 + j][2])
                for k in range(NK):
                    m = mm(bank, MT[:, k, 128 * t:128 * t + 128], wx[2 + j][1][:, k, :], k == 0, k == 7)
                z = P(m)
                V.wait(z)
                e2 = V(vec.tensor_copy(VX[:, t, 512 * j:512 * j + 512], bank))
                GB.free(gi, e2)
            W.free(wx[2 + j][0], (P.sem, P.n))
        t_kvx = (e, e2)
        wq = [wload([(w_xq_2[0][:, 512 * j:512 * j + 512], 0)], 512) for j in range(2)]
        w_o = [wload([(w_xo_2[0][:, 512 * j:512 * j + 512], 0)], 512) for j in range(2)]
        q_ready = []
        for j in range(2):
            for c in range(4):
                for n in range(2):
                    gi, bank = GB.take(P)
                    P.wait(wq[j][2])
                    for k in range(NK):
                        m = mm(bank, wq[j][1][:, k, 128 * c:128 * c + 128], HT[:, k, 512 * n:512 * n + 512],
                               k == 0, k == 7)
                    z = P(m)
                    C.wait(z)
                    e = C(act.activation(OT[:, 4 * j + c, 512 * n:512 * n + 512], bank, ACT.Copy, scale=1.0 / 16.0))
                    GB.free(gi, e)
            W.free(wq[j][0], (P.sem, P.n))
        P.wait(*t_kvx, e)
        PX = Slots([scr(32, 1024), scr(36, 1024)])
        PXT = Slots([scr(40, 1024), scr(44, 1024)])
        OX = Slots([scr(48, 1024), XBa[0]])

        def cross(t):
            si, sc = yield from SB.get(P)
            for h in range(4):
                for k in range(2):
                    m = mm(sc[:, 256 * h:256 * h + 256], OT[:, 2 * h + k, 128 * t:128 * t + 128],
                           KX[:, 2 * h + k, :], k == 0, k == 1)
            z = P(m)
            yield
            V.wait(z)
            s = ent8[t % 3]
            a = V(vec.tensor_reduce(s[:, 0:4], sc.rearrange("p (h c) -> p h c", h=4), AXX, MAX, negate=True))
            yield
            pi, px = yield from PX.get(C)
            C.wait(a)
            for h in range(4):
                e = C(act.activation(px[:, 256 * h:256 * h + 256], sc[:, 256 * h:256 * h + 256], ACT.Exp,
                                     bias=s[:, h:h + 1], accum_out=s[:, 4 + h:5 + h]))
            SB.free(si, e)
            yield
            V.wait(e)
            rl = V(vec.reciprocal(s[:, 8:12], s[:, 4:8]))
            ti_, pxt = yield from PXT.get(C, V)
            toks = yield from to_feature_major(px, pxt.rearrange("p (k s) -> p k s", k=8), e, t % 2)
            PX.free(pi, toks[0])
            oi, ox = yield from OX.get(V)
            for h2 in range(2):
                gi, bank = yield from GB.get(P)
                P.wait(*toks)
                for h in (2 * h2, 2 * h2 + 1):
                    for k in range(2):
                        m = mm(bank[:, 256 * (h % 2):256 * (h % 2) + 256], pxt[:, 256 * h + 128 * k:256 * h + 128 * k + 128],
                               VX[:, k, 256 * h:256 * h + 256], k == 0, k == 1)
                p = P(m)
                V.wait(p)
                for h in (2 * h2, 2 * h2 + 1):
                    f = V(vec.tensor_scalar(ox[:, 256 * h:256 * h + 256], bank[:, 256 * (h % 2):256 * (h % 2) + 256],
                                            s[:, 8 + h:9 + h], None, MUL))
                GB.free(gi, f)
                yield
            PXT.free(ti_, p)
            toks = yield from to_feature_major(ox, cols(OT, t), f, t % 2)
            OX.free(oi, toks[0])
            ot_ready[t] = toks[1:]

        ent8 = [stats(12) for _ in range(3)]
        run(pipeline([cross(t) for t in range(NT)], 4))
        all_engines_meet()
        reuse_x()
        GN, BN = scr(44, 1024), scr(48, 1024)
        t_g = once(bcast_row(GN, ln_x_g_2[0]), bcast_row(BN, ln_x_b_2[0]))
        Y.wait(*x1_done)
        for t in range(3):
            xload[t] = load_x(x3, t)
        RW = scr(0, 128).rearrange("p (k c) -> p k c", k=8)
        RBs = scr(0.5, 16)
        IO = scr(0.5625, 128)
        t_r = once((RW, router_w_2.rearrange("(k p) c -> p k c", p=128)), bcast_row(RBs, router_bias_2),
                   (IO, cst[:, C_N:C_N + 128]))
        def expert_gu(e_):
            return wload([(w_gate_2[0][e_], 0), (w_up_2[0][e_], 256)], 512)

        gus = {}
        r_bank = [*GB.take(P), None]

        def after_cross(t):
            yield from after_ln(t, w_o, x3, x4, GN, BN, t_g)
            if t in (4, 5):
                gus[t - 4] = expert_gu(t - 4)
            yield
            P.wait(t_r, *ht_ready[t])
            for k in range(NK):
                m = mm(r_bank[1][:, 16 * t:16 * t + 16], HT[:, k, 128 * t:128 * t + 128], RW[:, k, :], k == 0, k == 7)
            r_bank[2] = P(m)

        run(pipeline([after_cross(t) for t in range(NT)], 3))
        for w in w_o:
            W.free(w[0], (P.sem, P.n))
        x4_done = stores()

        WDb = [scr(24, 2048), scr(32, 2048)]
        WD = Slots(WDb)
        c_d = [Counter(sem()), Counter(sem())]

        def expert_down(e_):
            i, buf = WD.take(Y)
            d = buf.rearrange("p (k c) -> p k c", k=2)
            return (i, d, c_d[i](sync.dma_start(d, w_down_2[0][e_].rearrange("(k p) c -> p k c", p=128))))

        gus.update({e_: expert_gu(e_) for e_ in range(2, 4)})
        downs = {e_: expert_down(e_) for e_ in range(2)}
        gi, bank, z = r_bank
        r_at = [288]

        def rt(n):
            r_at[0] += n
            assert r_at[0] <= 24 * KW
            return SCR[:, r_at[0] - n:r_at[0]]

        SCO, SEL_, GWt, CH = rt(128), rt(128), rt(128), rt(128)
        C.wait(z)
        e = C(act.activation(SCO, bank[:, 0:128], ACT.Exp, scale=-1.0))
        GB.free(gi, e)
        V.wait(e, t_r)
        V(vec.tensor_scalar(SCO, SCO, 1.0, None, ADD))
        V.own()
        V(vec.reciprocal(SCO, SCO))
        V.own()

        def v3(a, c):
            return a.rearrange("p (t c) -> p t c", c=c)

        V(vec.tensor_tensor(v3(SEL_, 16), v3(SCO, 16), RBs.rearrange("p (a c) -> p a c", a=1).to_broadcast([128, 8, 16]), ADD))
        V.own()
        sv = v3(SEL_, 4)

        def lane(a, i):
            return v3(a, 4)[:, :, i]

        M1, N1, M2, N2, TT = [rt(32) for _ in range(5)]
        V(vec.tensor_tensor(M1, sv[:, :, 0], sv[:, :, 1], MAX))
        V(vec.tensor_tensor(N1, sv[:, :, 0], sv[:, :, 1], MIN))
        V(vec.tensor_tensor(M2, sv[:, :, 2], sv[:, :, 3], MAX))
        V(vec.tensor_tensor(N2, sv[:, :, 2], sv[:, :, 3], MIN))
        V.own()
        V(vec.tensor_tensor(TT, M1, M2, MIN))
        V(vec.tensor_tensor(N1, N1, N2, MAX))
        V(vec.tensor_tensor(M1, M1, M2, MAX))
        V.own()
        V(vec.tensor_tensor(TT, TT, N1, MAX))
        V.own()
        V(vec.tensor_tensor(TT, M1, TT, ADD))
        V.own()
        GM = rt(8)
        V(vec.tensor_reduce(GM, v3(TT, 4), AXX, MAX))
        V.own()
        EQ, NE, IGr, FR = rt(32), rt(32), rt(32), rt(16)
        V(vec.tensor_tensor(v3(EQ, 4), v3(TT, 4), v3(GM, 1).to_broadcast([128, 8, 4]), ALU.is_equal))
        t_ne = V(vec.tensor_tensor(v3(NE, 4), v3(TT, 4), v3(GM, 1).to_broadcast([128, 8, 4]), ALU.is_lt))
        BT, RK = rt(384), rt(128)
        b4 = BT.rearrange("p (g i j) -> p g i j", i=4, j=3)
        s4 = SEL_.rearrange("p (g i) -> p g i", i=4)
        for i in range(3):
            n = 3 - i
            one = s4[:, :, i:i + 1].to_broadcast([128, 32, n])
            V(vec.tensor_tensor(b4[:, :, i + 1:4, i], one, s4[:, :, i + 1:4], ALU.is_ge))
            V(vec.tensor_tensor(b4[:, :, i, i:3], s4[:, :, i + 1:4], one, ALU.is_gt))
        V.wait(t_ne)
        V(vec.tensor_tensor(FR[:, 0:8], lane(NE, 0), lane(NE, 1), MUL))
        V(vec.tensor_copy(lane(IGr, 0), lane(EQ, 0)))
        V(vec.tensor_tensor(lane(IGr, 1), lane(EQ, 1), lane(NE, 0), MUL))
        V.own()
        V(vec.tensor_reduce(RK, BT.rearrange("p (g j) -> p g j", j=3), AXX, ADD))
        V(vec.tensor_tensor(lane(IGr, 2), lane(EQ, 2), FR[:, 0:8], MUL))
        V(vec.tensor_tensor(FR[:, 8:16], FR[:, 0:8], lane(NE, 2), MUL))
        V.own()
        V(vec.tensor_tensor(lane(IGr, 3), lane(EQ, 3), FR[:, 8:16], MUL))
        V.own()
        V(vec.scalar_tensor_tensor(v3(CH, 4), v3(RK, 4), 1.5, v3(IGr, 1).to_broadcast([128, 32, 4]), ALU.is_lt, MUL))
        gw3 = v3(GWt, 16)

        ONE = rt(128)
        V(vec.memset(ONE, 1.0))
        V.own()
        gi, bank = GB.take(P)
        P.wait((V.sem, V.n))
        mm(bank[:, 0:128], CST[:, C_TR:C_TR + 128], CH, True, True)
        z = P(mm(bank[:, 128:256], ONE, CH, True, True))
        V.wait(z)
        PRE, POS = rt(144), rt(128)
        V(vec.memset(PRE[:, 0:16], 0.0))
        for t in range(NT):
            V.own()
            V(vec.tensor_tensor(PRE[:, 16 * t + 16:16 * t + 32], PRE[:, 16 * t:16 * t + 16],
                                bank[:, 128 + 16 * t:144 + 16 * t], ADD))
        V.own()
        e = V(vec.tensor_tensor(POS, PRE[:, 0:128], bank[:, 0:128], ADD))
        GB.free(gi, e)
        V.own()
        V(vec.tensor_scalar(POS, POS, float(CAP - 1), None, MIN))
        SLOT, TMP, FAR = rt(128), rt(128), rt(128)
        D12, COL, LO, G1, G2, MXC = rt(16), rt(16), rt(16), rt(8), rt(8), rt(1)
        eb = CST[:, C_EB:C_EB + 16].rearrange("p (a c) -> p a c", a=1).to_broadcast([128, 8, 16])
        V(vec.tensor_scalar(FAR, CH, -65536.0, 65536.0, MUL, ADD))
        V.own()
        V(vec.tensor_tensor(v3(SLOT, 16), v3(POS, 16), eb, ADD))
        V.own()
        V(vec.tensor_tensor(FAR, FAR, SLOT, ADD))
        V(vec.tensor_tensor(TMP, SLOT, CH, MUL))
        V.own()
        V(vec.tensor_reduce(D12[:, 0:8], v3(FAR, 16), AXX, MIN))
        V(vec.tensor_reduce(D12[:, 8:16], v3(TMP, 16), AXX, MAX))
        V.own()
        V(vec.tensor_scalar(COL, D12, 1.0 / 128.0, -0.49609375, MUL, ADD))
        V.own()
        V(vec.tensor_scalar(COL, COL, MAGIC, None, ADD))
        V.own()
        V(vec.tensor_scalar(COL, COL, MAGIC, None, SUB))
        V.own()
        V(vec.scalar_tensor_tensor(LO, COL, -128.0, D12, MUL, ADD))
        ROW, BLK = rt(2048), rt(512)
        V(vec.tensor_tensor(v3(BLK, 32), IO[:, 0:32].rearrange("p (a c) -> p a c", a=1).to_broadcast([128, 16, 32]),
                            v3(COL, 1).to_broadcast([128, 16, 32]), ALU.is_equal))
        V.own()
        gi, bank = GB.take(P)
        for j in range(16):
            c = V(vec.tensor_scalar(ROW[:, 128 * j:128 * j + 128], IO, LO[:, j:j + 1],
                                    CST[:, C_TI + j % 8:C_TI + j % 8 + 1], ALU.is_equal, MUL))
            P.wait(c)
            m = mm(bank[:, 0:32], ROW[:, 128 * j:128 * j + 128], BLK[:, 32 * j:32 * j + 32], j == 0, j == 15)
        z = P(m)
        V.wait(z)
        t_idx = V(vec.tensor_scalar(IDX[:, :], bank[:, 0:32], float(S - 1), None, MIN))
        GB.free(gi, t_idx)

        V(vec.tensor_tensor(GWt, SCO, CH, MUL))
        V(vec.tensor_reduce(MXC, PRE[:, 128:144], AXX, MAX))
        V.own()
        t_flag = V(vec.tensor_scalar(FLG[:, :], MXC, float(LIMIT), None, ALU.is_gt))
        V(vec.tensor_reduce(GM, v3(GWt, 16), AXX, ADD))
        V.own()
        V(vec.reciprocal(GM, GM))
        V.own()
        V(vec.tensor_tensor(v3(GWt, 16), v3(GWt, 16), v3(GM, 1).to_broadcast([128, 8, 16]), MUL))
        for i_ in range(2):
            V(vec.tensor_tensor(v3((TMP, FAR)[i_], 16), v3(SLOT, 16),
                                v3(D12[:, 8 * i_:8 * i_ + 8], 1).to_broadcast([128, 8, 16]), ALU.is_equal))
        V.own()
        for i_ in range(2):
            V(vec.tensor_tensor((TMP, FAR)[i_], (TMP, FAR)[i_], GWt, MUL))
        V.own()
        for i_ in range(2):
            V(vec.tensor_reduce((G1, G2)[i_], v3((TMP, FAR)[i_], 16), AXX, ADD))
        t_di = V(vec.tensor_copy(DI[:, :], D12))

        all_engines_meet()
        GEX = Slots([scr(40, 512), scr(42, 512)])
        HTs = Slots([scr(44, 512), scr(46, 512)])
        YS = Slots([scr(48, 1024), scr(52, 1024), scr(24 - 4, 1024)])
        OTf = [OT[:, k, :] for k in range(8)]
        XG = Slots(OTf[0:4])
        XT = Slots([A[:, 8192 + 4096 + 2048 * i:8192 + 4096 + 2048 * i + 2048] for i in range(2)])
        c_g = [Counter(sem()) for _ in range(4)]
        c_ys = [Counter(sem()) for _ in range(3)]
        G.wait(*x4_done, t_idx)
        Y.wait(*x4_done)
        reuse_x()
        for t in range(3):
            xload[t] = load_x(x4, t)

        YA = []
        c_ya = [Counter(sem()) for _ in range(NT)]
        c_yb = [Counter(sem()) for _ in range(NT)]
        FIRST = 3

        def rows(c, dst, src, j):
            return c(pool.indirect_dma_start(
                out=dst, out_offset=None, in_=src,
                in_offset=bass.IndirectOffsetOnAxis(ap=DI[:, j:j + 1].bitcast(mybir.dt.uint32), axis=0)))

        def first_rows():
            G.wait(t_di, *[(c.sem, c.n) for c in c_ys])
            for t in range(NT):
                if t % 4 == 0:
                    buf = W.take(G)[1]
                YA.append(buf[:, 1024 * (t % 4):1024 * (t % 4) + 1024])
            for t in range(FIRST):
                rows(c_ya[t], YA[t], slot_out[0:15 * CAP, :], t)

        def expert(e_):
            w = gus[e_]
            xi, xt = yield from XT.get(C, V)
            xt = xt.rearrange("p (k s) -> p k s", k=8)
            ready = []
            for b in range(2):
                gi_, xg = yield from XG.get(G)
                j = 2 * e_ + b
                t_x = c_g[gi_](pool.indirect_dma_start(
                    out=xg, out_offset=None, in_=x4,
                    in_offset=bass.IndirectOffsetOnAxis(ap=IDX[:, j:j + 1].bitcast(mybir.dt.uint32), axis=0)))
                yield
                toks = yield from to_feature_major(xg, xt[:, :, 128 * b:128 * b + 128], t_x, b)
                XG.free(gi_, toks[0])
                ready += toks[1:]
            si, sb2 = yield from SB.get(P)
            P.wait(w[2], *ready)
            for m_ in range(4):
                for k in range(NK):
                    m = mm(sb2[:, 256 * m_:256 * m_ + 256], w[1][:, k, 128 * m_:128 * m_ + 128], xt[:, k, :],
                           k == 0, k == 7)
                if m_ == 1:
                    z0 = P(m)
                    yield
            z = P(m)
            W.free(w[0], z)
            if e_ + 4 < 16:
                gus[e_ + 4] = expert_gu(e_ + 4)
            XT.free(xi, z)
            ei, ge = yield from GEX.get(C)
            hi, ht = yield from HTs.get(V)
            C.wait(z0)
            a = C(act.activation(ge, sb2[:, 0:512], ACT.Exp, scale=-1.0))
            V.wait(a)
            V(vec.tensor_scalar(ge, ge, 1.0, None, ADD))
            V.own()
            V(vec.reciprocal(ge, ge))
            V.own()
            V(vec.tensor_tensor(ge, ge, sb2[:, 0:512], MUL))
            V.own()
            V.wait(z)
            c = V(vec.tensor_tensor(ht, ge, sb2[:, 512:1024], MUL))
            GEX.free(ei, c)
            SB.free(si, c)
            yield
            while e_ not in downs:
                yield
            wd = downs[e_]
            for b in range(2):
                si, sb2 = yield from SB.get(P)
                P.wait(c, wd[2])
                for n in range(2):
                    for k in range(2):
                        m = mm(sb2[:, 512 * n:512 * n + 512], ht[:, 256 * k + 128 * b:256 * k + 128 * b + 128],
                               wd[1][:, k, 512 * n:512 * n + 512], k == 0, k == 1)
                p = P(m)
                yi, ys = yield from YS.get(C, V)
                C.wait(p)
                V.wait(p)
                a1 = C(act.activation(ys[:, 0:512], sb2[:, 0:512], ACT.Copy))
                a2 = V(vec.tensor_copy(ys[:, 512:1024], sb2[:, 512:1024]))
                SB.free(si, a1, a2)
                Y.wait(a1, a2)
                j = 2 * e_ + b
                YS.free(yi, c_ys[yi](sync.dma_start(slot_out[128 * j:128 * j + 128, :], ys)))
                yield
            HTs.free(hi, p)
            WD.free(wd[0], p)
            if e_ + 2 < 16:
                downs[e_ + 2] = expert_down(e_ + 2)
            if e_ == 14:
                first_rows()

        run(pipeline((expert(e_) for e_ in range(16)), 4))
        t_ys = [(c.sem, c.n) for c in c_ys]
        t_xg = [(c.sem, c.n) for c in c_g]
        NEWG = (G1, G2)

        def every_token_every_expert():
            V, C, P, G, Y = [Engine(e_, sem()) for e_ in (vec, act, pe, pool, sync)]
            before = [*t_main, *t_ys, *t_xg, *[(c.sem, c.n) for c in c_ya]]
            for e_ in (V, C, P, G, Y):
                e_.wait(*before)
            W = Slots(WR)
            c_w = [Counter(sem()) for _ in range(4)]
            SB = Slots([PS[:, 0:1024], PS[:, 1024:2048]])
            TB = Slots([PS[:, 2048:2560], PS[:, 2560:3072]])
            GB = Slots([PS[:, 3072:3584], PS[:, 3584:4096]])
            WD = Slots(WDb)
            c_d = [Counter(sem()), Counter(sem())]
            HS = Slots([scr(40 + 2 * i, 512) for i in range(2)])
            HTs = Slots([scr(44 + i, 256) for i in range(4)])
            c_y = Counter(sem())
            for t in range(NT):
                V(vec.memset(OT[:, t, :], 0.0))
            y_last = [(V.sem, V.n)] * NT
            ew = {}

            def load(e_):
                i, buf = W.take(Y)
                v = buf.rearrange("p (k c) -> p k c", k=8)
                c_w[i](sync.dma_start(v[:, :, 0:256], w_gate_2[0][e_].rearrange("(k p) c -> p k c", p=128)))
                tw = c_w[i](sync.dma_start(v[:, :, 256:512], w_up_2[0][e_].rearrange("(k p) c -> p k c", p=128)))
                di, dbuf = WD.take(Y)
                d = dbuf.rearrange("p (k c) -> p k c", k=2)
                td = c_d[di](sync.dma_start(d, w_down_2[0][e_].rearrange("(k p) c -> p k c", p=128)))
                ew[e_] = (i, v, tw, di, d, td)

            def block(e_, t):
                wi_, w, tw, di, wd, td = ew[e_]
                gi, bank = yield from GB.get(P)
                P.wait(tw)
                for k in range(NK):
                    m = mm(bank, HT[:, k, 128 * t:128 * t + 128], w[:, k, :], k == 0, k == 7)
                z = P(m)
                if t == NT - 1:
                    W.free(wi_, z)
                yield
                hi, hs = yield from HS.get(C, V)
                C.wait(z)
                a = C(act.activation(hs[:, 256:512], bank[:, 0:256], ACT.Exp, scale=-1.0))
                yield
                V.wait(a)
                V(vec.tensor_scalar(hs[:, 256:512], hs[:, 256:512], 1.0, None, ADD))
                V.own()
                V(vec.reciprocal(hs[:, 256:512], hs[:, 256:512]))
                V.own()
                V(vec.scalar_tensor_tensor(hs[:, 0:256], hs[:, 256:512], gw3[:, t, e_:e_ + 1], bank[:, 0:256],
                                           MUL, MUL))
                V.own()
                b = V(vec.tensor_tensor(hs[:, 0:256], hs[:, 0:256], bank[:, 256:512], MUL))
                GB.free(gi, b)
                yield
                ti, tb = yield from TB.get(P)
                P.wait(b)
                for k in range(2):
                    m = tr(tb[:, 128 * k:128 * k + 128], hs[:, 128 * k:128 * k + 128], ident)
                p = P(m)
                HS.free(hi, p)
                hti, ht = yield from HTs.get(C)
                C.wait(p)
                c = C(act.activation(ht, tb[:, 0:256], ACT.Copy))
                TB.free(ti, c)
                yield
                si, sb2 = yield from SB.get(P)
                P.wait(c, td)
                for n in range(2):
                    for k in range(2):
                        m = mm(sb2[:, 512 * n:512 * n + 512], ht[:, 128 * k:128 * k + 128],
                               wd[:, k, 512 * n:512 * n + 512], k == 0, k == 1)
                p = P(m)
                HTs.free(hti, p)
                if t == NT - 1:
                    WD.free(di, p)
                    if e_ + 2 < 16:
                        load(e_ + 2)
                yield
                V.wait(p, y_last[t])
                y_last[t] = V(vec.tensor_tensor(OT[:, t, :], OT[:, t, :], sb2, ADD))
                SB.free(si, y_last[t])

            load(0)
            load(1)
            run(pipeline((block(e_, t) for e_ in range(16) for t in range(NT)), 4))
            V.own()
            V(vec.tensor_copy(DI[:, 0:8], CST[:, C_TI:C_TI + 8]))
            V(vec.tensor_copy(DI[:, 8:16], CST[:, C_TI:C_TI + 8]))
            V(vec.memset(G1, 1.0))
            for t in range(FIRST):
                V(vec.tensor_copy(YA[t], OT[:, t, :]))
            t_end = V(vec.memset(G2, 0.0))
            Y.wait(t_end)
            for t in range(NT):
                t_y = c_y(sync.dma_start(slot_out[128 * t:128 * t + 128, :], OT[:, t, :]))
            for e_ in (V, C, P, G, Y):
                e_.wait(t_end, t_y, (C.sem, C.n), (P.sem, P.n))

        t_main = [(e_.sem, e_.n) for e_ in (P, C, V)]
        for e_ in (V, C, P, G, Y):
            e_.wait(t_flag)
        over = nc.values_load(FLG[0:1, 0:1], min_val=0, max_val=1)
        with nc.If(over == 1):
            every_token_every_expert()

        all_engines_meet()
        XN.freed = [()] * 2
        XN.at = 0
        GN, BN = scr(44, 1024), scr(48, 1024)
        t_g = once(bcast_row(GN, ln_moe_g_2[0]), bcast_row(BN, ln_moe_b_2[0]))
        G.wait(*t_ys, t_di)
        for t in range(NT):
            rows(c_yb[t], OTf[t], slot_out, 8 + t)
            if t + FIRST < NT:
                rows(c_ya[t + FIRST], YA[t + FIRST], slot_out, t + FIRST)

        def last(t):
            i, buf, tx = xload[t]
            ya, yb = YA[t], OTf[t]
            s = lnst[t % 3]
            C.wait((c_ya[t].sem, c_ya[t].n))
            a = C(act.activation(ya, ya, ACT.Identity, scale=G1[:, t:t + 1]))
            yield
            V.wait(tx, (c_yb[t].sem, c_yb[t].n), a)
            V(vec.scalar_tensor_tensor(ya, yb, G2[:, t:t + 1], ya, MUL, ADD))
            V.own()
            r = V(vec.scalar_tensor_tensor(buf, buf, ALPHA, ya, MUL, ADD))
            V.own()
            for h in range(2):
                V(vec.bn_stats(s[:, 6 * h:6 * h + 6], buf[:, 512 * h:512 * h + 512]))
            V.own()
            V(vec.bn_aggr(s[:, 12:14], s[:, 0:12]))
            V.own()
            b = V(vec.tensor_scalar(s[:, 14:15], s[:, 13:14], LN_EPS, None, ADD))
            yield
            rsqrt(s[:, 14:15], s[:, 15:16], b)
            b = V(vec.scalar_tensor_tensor(s[:, 16:17], s[:, 12:13], -1.0, s[:, 15:16], MUL, MUL))
            ni, xn = yield from XN.get(C)
            C.wait(b)
            n = C(act.activation(xn, buf, ACT.Identity, scale=s[:, 15:16], bias=s[:, 16:17]))
            XB.free(i, n)
            if t + 3 < NT:
                xload[t + 3] = load_x(x4, t + 3)
            yield
            V.wait(n, t_g)
            n = V(vec.tensor_tensor(xn, xn, GN, MUL))
            V.own()
            yield
            V.wait(n, t_g)
            n = V(vec.tensor_tensor(xn, xn, BN, ADD))
            Y.wait(n)
            st = c_sn[ni](sync.dma_start(out[0][128 * t:128 * t + 128, :], xn))
            XN.free(ni, st)
            yield

        run(pipeline([last(t) for t in range(NT)], 3))
        Y.wait(*stores())


_INS = ['x', 'positions', 'e_g_in', 'e_w_in', 'e_g_q_a', 'e_w_q_up', 'e_g_kv_a', 'e_w_kv_up', 'e_sinks', 'e_w_out',
        'o_g_in', 'o_w_in', 'o_b_f', 'o_w_out', 'g_final', 'mem_2', 'w_in_2', 'b_i_2', 'b_f_2', 'conv_qk_2',
        'head_norm_g_2', 'pool_w_2', 'pool_scale_2', 'w_mix_out_2', 'ln_mix_g_2', 'ln_mix_b_2', 'w_xq_2', 'w_xkv_2',
        'w_xo_2', 'ln_x_g_2', 'ln_x_b_2', 'router_w_2', 'router_bias_2', 'w_gate_2', 'w_up_2', 'w_down_2',
        'ln_moe_g_2', 'ln_moe_b_2']


def constants():
    import numpy as np

    c = np.zeros((128, C_N + 128), np.float32)
    c[:, C_N:] = np.arange(128)[None, :]
    c[:, C_ID:C_ID + 128] = np.eye(128)
    q = np.arange(128)
    c[:, C_MQ:C_MQ + 128] = np.where(q[None, :] > q[:, None], -BIG, 0.0)
    c[:, C_MT:C_MT + 128] = np.where(q[:, None] > q[None, :], -BIG, 0.0)
    k = np.arange(256)
    dist = 128 + q[:, None] - k[None, :]
    c[:, C_DM:C_DM + 256] = np.where((dist >= 0) & (dist < 128), dist, BIG)
    for g in range(4):
        c[:, C_IC + 16 * g:C_IC + 16 * g + 16] = 1.0 / np.minimum(np.arange(1, 17), 2 ** (g + 1))
    c[:, C_IF:C_IF + 16] = (1.0 / (np.float32(10000.0) ** (np.arange(0, 32, 2, dtype=np.float32) / np.float32(32))))
    c[:, C_TR:C_TR + 128] = q[:, None] < q[None, :]
    c[:, C_EB:C_EB + 16] = CAP * np.arange(16)
    c[:, C_TI:C_TI + 8] = q[:, None] + 128 * np.arange(8)[None, :]
    for h in range(4):
        c[h, C_BD + 8 * h:C_BD + 8 * h + 8] = 1.0
    return c


def kernel(**inputs):
    import numpy as _np
    import concourse.bacc as _bacc
    from concourse import mybir as _mybir
    from concourse.bass_utils import run_bass_kernel_spmd as _run

    nc = _bacc.Bacc("TRN2", target_bir_lowering=False, num_devices=1)
    arrays, args = {}, []
    for name in _INS:
        a = _np.ascontiguousarray(inputs[name])
        arrays[f"in_{name}_dram"] = a
        args.append(nc.dram_tensor(f"in_{name}_dram", a.shape, _mybir.dt.from_np(a.dtype), kind="ExternalInput").ap())
    a = constants()
    arrays["in_tables_dram"] = a
    args.append(nc.dram_tensor("in_tables_dram", a.shape, _mybir.dt.from_np(a.dtype), kind="ExternalInput").ap())
    args.append(nc.dram_tensor("out_0_dram", (1, S, D), F32, kind="ExternalOutput").ap())
    program(nc, *args)
    r = _run(nc, [arrays], core_ids=[0])
    return r.results[0]["out_0_dram"]
```
